# Optimizing a Trainium2 kernel written in Bass

```python
import math
import jax
import jax.numpy as jnp
from jax import lax
import numpy as np
import jax, jax.numpy as jnp

D_MODEL = 1024
BATCH = 1
SEQ = 512
DEPTH = 1

CHUNK = 64
Q_BLOCK = 128
EPS = 1e-6
NEG_INF = -1e30

N_ATTN_HEADS = 8
HEAD_DIM = D_MODEL // (2 * N_ATTN_HEADS)
V_HEAD_DIM = 2 * HEAD_DIM
QK_WIDTH = N_ATTN_HEADS * 2 * HEAD_DIM
ATTN_WIDTH = N_ATTN_HEADS * V_HEAD_DIM

D_RNN = (5 * D_MODEL) // 4
RNN_BLOCK = 64
N_RNN_BLOCKS = D_RNN // RNN_BLOCK
CONV_WIDTH = 4
RG_C = 8.0

N_BRANCH = 2
IN_SPLITS = (QK_WIDTH, 2 * QK_WIDTH, 2 * QK_WIDTH + ATTN_WIDTH,
             2 * QK_WIDTH + ATTN_WIDTH + D_RNN, 2 * QK_WIDTH + ATTN_WIDTH + 2 * D_RNN)
IN_COLS = 2 * QK_WIDTH + ATTN_WIDTH + 2 * D_RNN + N_BRANCH * D_MODEL

PEER_HEADS = 8
PEER_N_KEYS = 128
PEER_N_EXPERTS = PEER_N_KEYS ** 2
PEER_QDIM = 256
PEER_HALF = PEER_QDIM // 2
PEER_TOPK = 16
PEER_BLOCK = 128


def rms_norm(x, g):
    xf = x.astype(jnp.float32)
    y = xf * lax.rsqrt(jnp.mean(xf * xf, axis=-1, keepdims=True) + EPS)
    return (y * g.astype(jnp.float32)).astype(x.dtype)

def diff_attention(q, k, v, q_norm_g, k_norm_g, lambda_q1, lambda_k1, lambda_q2, lambda_k2,
                   subln_g, lam_init):
    b, s = q.shape[0], q.shape[1]
    n_blk = s // Q_BLOCK
    q = rms_norm(q, q_norm_g)
    k = rms_norm(k, k_norm_g)
    lam = (jnp.exp(jnp.sum(lambda_q1.astype(jnp.float32) * lambda_k1.astype(jnp.float32)))
           - jnp.exp(jnp.sum(lambda_q2.astype(jnp.float32) * lambda_k2.astype(jnp.float32)))
           + lam_init)
    scale = HEAD_DIM ** -0.5
    key_chunk = jnp.arange(s) // CHUNK
    q_blocks = q.reshape(b, n_blk, Q_BLOCK, N_ATTN_HEADS, 2, HEAD_DIM).transpose(1, 0, 2, 3, 4, 5)

    def one_block(args):
        q_blk, blk = args
        scores = jnp.einsum('bqhcd,bkhcd->bhcqk', q_blk, k).astype(jnp.float32) * scale
        q_chunk = (blk * Q_BLOCK + jnp.arange(Q_BLOCK)) // CHUNK
        visible = key_chunk[None, :] <= q_chunk[:, None]
        scores = jnp.where(visible, scores, NEG_INF)
        probs = jax.nn.softmax(scores, axis=-1)
        diff = probs[:, :, 0] - lam * probs[:, :, 1]
        return jnp.einsum('bhqk,bkhd->bqhd', diff.astype(v.dtype), v)

    o = lax.map(one_block, (q_blocks, jnp.arange(n_blk)))
    o = o.transpose(1, 0, 2, 3, 4).reshape(b, s, N_ATTN_HEADS, V_HEAD_DIM)
    o = rms_norm(o, subln_g) * (1.0 - lam_init)
    return o.reshape(b, s, ATTN_WIDTH)

def causal_depthwise_conv(x, w, bias):
    s = x.shape[1]
    xp = jnp.pad(x, ((0, 0), (CONV_WIDTH - 1, 0), (0, 0)))
    y = bias
    for tap in range(CONV_WIDTH):
        y = y + xp[:, tap:tap + s] * w[tap]
    return y

def rg_lru(x, w_a, b_a, w_x, b_x, rg_lambda):
    b, s, _ = x.shape
    xb = x.reshape(b, s, N_RNN_BLOCKS, RNN_BLOCK)
    gate_r = jax.nn.sigmoid(jnp.einsum('bsgi,gij->bsgj', xb, w_a).reshape(b, s, D_RNN) + b_a)
    gate_i = jax.nn.sigmoid(jnp.einsum('bsgi,gij->bsgj', xb, w_x).reshape(b, s, D_RNN) + b_x)
    log_a = -RG_C * gate_r.astype(jnp.float32) * jax.nn.softplus(-rg_lambda.astype(jnp.float32))
    a = jnp.exp(log_a)
    mult = jnp.sqrt(-jnp.expm1(2.0 * log_a))
    u = mult * (gate_i * x).astype(jnp.float32)

    def combine(left, right):
        a_l, u_l = left
        a_r, u_r = right
        return a_l * a_r, a_r * u_l + u_r

    _, h = lax.associative_scan(combine, (a, u), axis=1)
    return h.astype(x.dtype)

def peer_ffn(h, w_q, sub_keys, u_tab, v_tab):
    b, s, d = h.shape
    tokens = h.reshape((b * s) // PEER_BLOCK, PEER_BLOCK, d)

    def one_block(hb):
        q = (hb @ w_q).reshape(PEER_BLOCK, PEER_HEADS, 2, PEER_HALF)
        sc = jnp.einsum('thcd,hcnd->thcn', q, sub_keys).astype(jnp.float32)
        s1, i1 = lax.top_k(sc[:, :, 0], PEER_TOPK)
        s2, i2 = lax.top_k(sc[:, :, 1], PEER_TOPK)
        cand_s = (s1[..., :, None] + s2[..., None, :]).reshape(PEER_BLOCK, PEER_HEADS, PEER_TOPK * PEER_TOPK)
        cand_i = (i1[..., :, None] * PEER_N_KEYS + i2[..., None, :]).reshape(PEER_BLOCK, PEER_HEADS, PEER_TOPK * PEER_TOPK)
        top_s, pos = lax.top_k(cand_s, PEER_TOPK)
        idx = jnp.take_along_axis(cand_i, pos, axis=-1)
        g = jax.nn.softmax(top_s, axis=-1)
        u = u_tab[idx]
        act = jax.nn.gelu(jnp.einsum('thkd,td->thk', u, hb))
        wts = (g * act.astype(jnp.float32)).astype(hb.dtype)
        v = v_tab[idx]
        return jnp.einsum('thk,thkd->td', wts, v)

    out = lax.map(one_block, tokens)
    return out.reshape(b, s, d)

def hybrid_block(x, lam_init, norm1_g, w_in, b_gate, q_norm_g, k_norm_g, lambda_q1, lambda_k1,
                 lambda_q2, lambda_k2, subln_g, conv_w, conv_b, w_rg_a, b_rg_a, w_rg_x, b_rg_x,
                 rg_lambda, w_br_attn, w_br_rnn, w_out, norm2_g, w_peer_q, peer_sub_keys,
                 peer_u, peer_v):
    b, s, _ = x.shape
    h = rms_norm(x, norm1_g)
    z = h @ w_in
    q, k, v, xr, yr, gate_logits = jnp.split(z, IN_SPLITS, axis=-1)
    q = q.reshape(b, s, N_ATTN_HEADS, 2, HEAD_DIM)
    k = k.reshape(b, s, N_ATTN_HEADS, 2, HEAD_DIM)
    v = v.reshape(b, s, N_ATTN_HEADS, V_HEAD_DIM)
    attn = diff_attention(q, k, v, q_norm_g, k_norm_g, lambda_q1, lambda_k1, lambda_q2,
                          lambda_k2, subln_g, lam_init)
    rnn = rg_lru(causal_depthwise_conv(xr, conv_w, conv_b), w_rg_a, b_rg_a, w_rg_x, b_rg_x,
                 rg_lambda) * jax.nn.gelu(yr)
    gates = jax.nn.sigmoid(gate_logits + b_gate).reshape(b, s, N_BRANCH, D_MODEL)
    merged = gates[:, :, 0] * (attn @ w_br_attn) + gates[:, :, 1] * (rnn @ w_br_rnn)
    x = x + merged @ w_out
    x = x + peer_ffn(rms_norm(x, norm2_g), w_peer_q, peer_sub_keys, peer_u, peer_v)
    return x

def first_inputs(seed: int = 0) -> dict:
    key = jax.random.key(seed)
    ks = jax.random.split(key, 26)
    L = DEPTH

    def nrm(k, shape, scale):
        return jax.random.normal(k, shape, jnp.float32) * scale

    a0 = jax.random.uniform(ks[17], (L, D_RNN), jnp.float32, 0.9, 0.999)
    return {
        'x': nrm(ks[0], (BATCH, SEQ, D_MODEL), 1.0),
        'norm1_g': 1.0 + nrm(ks[1], (L, D_MODEL), 0.02),
        'w_in': nrm(ks[2], (L, D_MODEL, IN_COLS), D_MODEL ** -0.5),
        'b_gate': nrm(ks[3], (L, N_BRANCH * D_MODEL), 0.02),
        'q_norm_g': 1.0 + nrm(ks[4], (L, HEAD_DIM), 0.02),
        'k_norm_g': 1.0 + nrm(ks[5], (L, HEAD_DIM), 0.02),
        'lambda_q1': nrm(ks[6], (L, HEAD_DIM), 0.1),
        'lambda_k1': nrm(ks[7], (L, HEAD_DIM), 0.1),
        'lambda_q2': nrm(ks[8], (L, HEAD_DIM), 0.1),
        'lambda_k2': nrm(ks[9], (L, HEAD_DIM), 0.1),
        'subln_g': 1.0 + nrm(ks[10], (L, V_HEAD_DIM), 0.02),
        'conv_w': nrm(ks[11], (L, CONV_WIDTH, D_RNN), CONV_WIDTH ** -0.5),
        'conv_b': nrm(ks[12], (L, D_RNN), 0.02),
        'w_rg_a': nrm(ks[13], (L, N_RNN_BLOCKS, RNN_BLOCK, RNN_BLOCK), RNN_BLOCK ** -0.5),
        'b_rg_a': nrm(ks[14], (L, D_RNN), 0.02),
        'w_rg_x': nrm(ks[15], (L, N_RNN_BLOCKS, RNN_BLOCK, RNN_BLOCK), RNN_BLOCK ** -0.5),
        'b_rg_x': nrm(ks[16], (L, D_RNN), 0.02),
        'rg_lambda': jnp.log(a0) - jnp.log1p(-a0),
        'w_br_attn': nrm(ks[18], (L, ATTN_WIDTH, D_MODEL), ATTN_WIDTH ** -0.5),
        'w_br_rnn': nrm(ks[19], (L, D_RNN, D_MODEL), D_RNN ** -0.5),
        'w_out': nrm(ks[20], (L, D_MODEL, D_MODEL), D_MODEL ** -0.5),
        'norm2_g': 1.0 + nrm(ks[21], (L, D_MODEL), 0.02),
        'w_peer_q': nrm(ks[22], (L, D_MODEL, PEER_HEADS * PEER_QDIM), D_MODEL ** -0.5),
        'peer_sub_keys': nrm(ks[23], (L, PEER_HEADS, 2, PEER_N_KEYS, PEER_HALF), PEER_HALF ** -0.5),
        'peer_u': nrm(ks[24], (L, PEER_N_EXPERTS, D_MODEL), D_MODEL ** -0.5),
        'peer_v': nrm(ks[25], (L, PEER_N_EXPERTS, D_MODEL), PEER_HEADS ** -0.5),
    }

def first_block(x, norm1_g, w_in, b_gate, q_norm_g, k_norm_g, lambda_q1, lambda_k1, lambda_q2,
              lambda_k2, subln_g, conv_w, conv_b, w_rg_a, b_rg_a, w_rg_x, b_rg_x, rg_lambda,
              w_br_attn, w_br_rnn, w_out, norm2_g, w_peer_q, peer_sub_keys, peer_u, peer_v):
    for layer in range(DEPTH):
        lam_init = 0.8 - 0.6 * math.exp(-0.3 * layer)
        x = hybrid_block(x, lam_init, norm1_g[layer], w_in[layer], b_gate[layer], q_norm_g[layer],
                         k_norm_g[layer], lambda_q1[layer], lambda_k1[layer], lambda_q2[layer],
                         lambda_k2[layer], subln_g[layer], conv_w[layer], conv_b[layer],
                         w_rg_a[layer], b_rg_a[layer], w_rg_x[layer], b_rg_x[layer],
                         rg_lambda[layer], w_br_attn[layer], w_br_rnn[layer], w_out[layer],
                         norm2_g[layer], w_peer_q[layer], peer_sub_keys[layer], peer_u[layer],
                         peer_v[layer])
    return x


MEM_LEN = 256
HEAD_DIM_2 = 64
ATTN_WIDTH_2 = D_MODEL // 2
N_Q_HEADS = ATTN_WIDTH_2 // HEAD_DIM_2
N_KV_HEADS = N_Q_HEADS // 4
Q_PER_KV = N_Q_HEADS // N_KV_HEADS
WINDOW = 128
BLOCK = 128
CONV_CH = D_MODEL // 4
CONV_WIDTH_2 = 31
MEM_WIDTH = D_MODEL // 4
N_MEM_HEADS = MEM_WIDTH // HEAD_DIM_2
MIX_WIDTH = ATTN_WIDTH_2 + CONV_CH + MEM_WIDTH
ROPE_THETA = 500000.0
ROPE_DIM = HEAD_DIM_2 // 4
D_FF = 256 * math.ceil(8 * D_MODEL / 3 / 256)

Q_COLS = N_Q_HEADS * HEAD_DIM_2
KV_COLS = N_KV_HEADS * HEAD_DIM_2
GLU_COLS = 2 * CONV_CH
MQ_COLS = N_MEM_HEADS * HEAD_DIM_2
IN_COLS_2 = Q_COLS + 2 * KV_COLS + GLU_COLS + MQ_COLS
SPLITS = [Q_COLS, Q_COLS + KV_COLS, Q_COLS + 2 * KV_COLS, Q_COLS + 2 * KV_COLS + GLU_COLS]


def rms_norm_2(x, g):
    xf = x.astype(jnp.float32)
    y = xf * lax.rsqrt(jnp.mean(xf * xf, axis=-1, keepdims=True) + EPS)
    return (y * g.astype(jnp.float32)).astype(x.dtype)

def layer_norm(x, g, b):
    xf = x.astype(jnp.float32)
    mu = jnp.mean(xf, axis=-1, keepdims=True)
    var = jnp.mean(jnp.square(xf - mu), axis=-1, keepdims=True)
    y = (xf - mu) * lax.rsqrt(var + EPS)
    return (y * g.astype(jnp.float32) + b.astype(jnp.float32)).astype(x.dtype)

def swiglu(x, w_gate, w_up, w_down):
    return (jax.nn.silu(x @ w_gate) * (x @ w_up)) @ w_down

def rope_partial(x, positions):
    half = ROPE_DIM // 2
    inv_freq = ROPE_THETA ** (-jnp.arange(half, dtype=jnp.float32) / half)
    ang = positions.astype(jnp.float32)[..., None] * inv_freq
    cos = jnp.cos(ang)[:, :, None, :]
    sin = jnp.sin(ang)[:, :, None, :]
    xr = x[..., :ROPE_DIM].astype(jnp.float32)
    x1, x2 = xr[..., :half], xr[..., half:]
    rot = jnp.concatenate([x1 * cos - x2 * sin, x2 * cos + x1 * sin], axis=-1).astype(x.dtype)
    return jnp.concatenate([rot, x[..., ROPE_DIM:]], axis=-1)

def sliding_window_attention(q, k, v, sinks):
    B, T = q.shape[0], q.shape[1]
    nb = T // BLOCK
    qb = q.reshape(B, nb, BLOCK, N_KV_HEADS, Q_PER_KV, HEAD_DIM_2)

    def with_prev(a):
        a = a.reshape(B, nb, BLOCK, N_KV_HEADS, HEAD_DIM_2)
        prev = jnp.pad(a, ((0, 0), (1, 0), (0, 0), (0, 0), (0, 0)))[:, :-1]
        return jnp.concatenate([prev, a], axis=2)

    kb, vb = with_prev(k), with_prev(v)
    s = jnp.einsum('bnqgrd,bnkgd->bngrqk', qb, kb).astype(jnp.float32) * (HEAD_DIM_2 ** -0.5)
    qi = jnp.arange(BLOCK)[:, None] + BLOCK
    ki = jnp.arange(2 * BLOCK)[None, :]
    rel = qi - ki
    band = (rel >= 0) & (rel < WINDOW)
    blk = jnp.arange(nb)[:, None, None]
    valid = band[None] & ((blk > 0) | (ki >= BLOCK)[None])
    s = jnp.where(valid[None, :, None, None], s, -jnp.inf)
    sink = sinks.astype(jnp.float32).reshape(N_KV_HEADS, Q_PER_KV)[None, None, :, :, None, None]
    m = jnp.maximum(jnp.max(s, axis=-1, keepdims=True), sink)
    p = jnp.exp(s - m)
    denom = jnp.sum(p, axis=-1, keepdims=True) + jnp.exp(sink - m)
    w = (p / denom).astype(v.dtype)
    o = jnp.einsum('bngrqk,bnkgd->bnqgrd', w, vb)
    return o.reshape(B, T, N_Q_HEADS * HEAD_DIM_2)

def memory_cross_attention(q, k, v):
    B, T = q.shape[0], q.shape[1]
    s = jnp.einsum('bthd,bmhd->bhtm', q, k).astype(jnp.float32) * (HEAD_DIM_2 ** -0.5)
    w = jax.nn.softmax(s, axis=-1).astype(v.dtype)
    o = jnp.einsum('bhtm,bmhd->bthd', w, v)
    return o.reshape(B, T, N_MEM_HEADS * HEAD_DIM_2)

def conformer_conv(u, w_dw, b_dw, g_ln, b_ln):
    a, gate = jnp.split(u, 2, axis=-1)
    h = a * jax.nn.sigmoid(gate)
    h = lax.conv_general_dilated(
        h, w_dw[:, None, :].astype(h.dtype), window_strides=(1,),
        padding=((CONV_WIDTH_2 - 1, 0),), dimension_numbers=('NWC', 'WIO', 'NWC'),
        feature_group_count=CONV_CH) + b_dw
    return jax.nn.silu(layer_norm(h, g_ln, b_ln))

def second_inputs(seed: int = 0) -> dict:
    key = jax.random.key(seed)
    ks = jax.random.split(key, 32)
    f32 = jnp.float32

    def w(k, shape, fan_in):
        return jax.random.normal(k, shape, f32) * (fan_in ** -0.5)

    def gain(k, shape):
        return 1.0 + 0.05 * jax.random.normal(k, shape, f32)

    L = DEPTH
    start = jax.random.randint(ks[2], (BATCH, 1), 0, 1024, dtype=jnp.int32)
    positions = start + jnp.arange(SEQ, dtype=jnp.int32)[None, :]
    return {
        "x": jax.random.normal(ks[0], (BATCH, SEQ, D_MODEL), f32),
        "mem": jax.random.normal(ks[1], (BATCH, MEM_LEN, D_MODEL), f32),
        "positions": positions,
        "g_ffn1": gain(ks[3], (L, D_MODEL)),
        "w_ffn1_gate": w(ks[4], (L, D_MODEL, D_FF), D_MODEL),
        "w_ffn1_up": w(ks[5], (L, D_MODEL, D_FF), D_MODEL),
        "w_ffn1_down": w(ks[6], (L, D_FF, D_MODEL), D_FF),
        "g_mix": gain(ks[7], (L, D_MODEL)),
        "w_in": w(ks[8], (L, D_MODEL, IN_COLS_2), D_MODEL),
        "g_q": gain(ks[9], (L, HEAD_DIM_2)),
        "g_k": gain(ks[10], (L, HEAD_DIM_2)),
        "sinks": 0.5 * jax.random.normal(ks[11], (L, N_Q_HEADS), f32),
        "w_dw": w(ks[12], (L, CONV_WIDTH_2, CONV_CH), CONV_WIDTH_2),
        "b_dw": 0.02 * jax.random.normal(ks[13], (L, CONV_CH), f32),
        "g_conv_ln": gain(ks[14], (L, CONV_CH)),
        "b_conv_ln": 0.02 * jax.random.normal(ks[15], (L, CONV_CH), f32),
        "g_mem": gain(ks[16], (L, D_MODEL)),
        "w_mem_kv": w(ks[17], (L, D_MODEL, 2 * MQ_COLS), D_MODEL),
        "g_mq": gain(ks[18], (L, HEAD_DIM_2)),
        "g_mk": gain(ks[19], (L, HEAD_DIM_2)),
        "w_out": w(ks[20], (L, MIX_WIDTH, D_MODEL), MIX_WIDTH),
        "g_ffn2": gain(ks[21], (L, D_MODEL)),
        "w_ffn2_gate": w(ks[22], (L, D_MODEL, D_FF), D_MODEL),
        "w_ffn2_up": w(ks[23], (L, D_MODEL, D_FF), D_MODEL),
        "w_ffn2_down": w(ks[24], (L, D_FF, D_MODEL), D_FF),
    }

def second_block(x, mem, positions, g_ffn1, w_ffn1_gate, w_ffn1_up, w_ffn1_down,
              g_mix, w_in, g_q, g_k, sinks, w_dw, b_dw, g_conv_ln, b_conv_ln,
              g_mem, w_mem_kv, g_mq, g_mk, w_out,
              g_ffn2, w_ffn2_gate, w_ffn2_up, w_ffn2_down):
    B, T = x.shape[0], x.shape[1]
    M = mem.shape[1]
    for l in range(DEPTH):
        x = x + 0.5 * swiglu(rms_norm_2(x, g_ffn1[l]), w_ffn1_gate[l], w_ffn1_up[l], w_ffn1_down[l])

        h = rms_norm_2(x, g_mix[l])
        proj = h @ w_in[l]
        q, k, v, u, mq = jnp.split(proj, SPLITS, axis=-1)
        q = q.reshape(B, T, N_Q_HEADS, HEAD_DIM_2)
        k = k.reshape(B, T, N_KV_HEADS, HEAD_DIM_2)
        v = v.reshape(B, T, N_KV_HEADS, HEAD_DIM_2)
        q = rope_partial(rms_norm_2(q, g_q[l]), positions)
        k = rope_partial(rms_norm_2(k, g_k[l]), positions)
        y_attn = sliding_window_attention(q, k, v, sinks[l])

        y_conv = conformer_conv(u, w_dw[l], b_dw[l], g_conv_ln[l], b_conv_ln[l])

        mkv = rms_norm_2(mem, g_mem[l]) @ w_mem_kv[l]
        mk, mv = jnp.split(mkv, 2, axis=-1)
        mq = rms_norm_2(mq.reshape(B, T, N_MEM_HEADS, HEAD_DIM_2), g_mq[l])
        mk = rms_norm_2(mk.reshape(B, M, N_MEM_HEADS, HEAD_DIM_2), g_mk[l])
        mv = mv.reshape(B, M, N_MEM_HEADS, HEAD_DIM_2)
        y_mem = memory_cross_attention(mq, mk, mv)

        x = x + jnp.concatenate([y_attn, y_conv, y_mem], axis=-1) @ w_out[l]

        x = x + 0.5 * swiglu(rms_norm_2(x, g_ffn2[l]), w_ffn2_gate[l], w_ffn2_up[l], w_ffn2_down[l])
    return x


def setup_inputs(seed=0):
    out = dict(first_inputs(seed))
    for name, value in second_inputs(seed + 1).items():
        if name != "x":
            out[name + "_2"] = value
    return out


def reference(
    x, norm1_g, w_in, b_gate, q_norm_g, k_norm_g, lambda_q1, lambda_k1, lambda_q2, lambda_k2,
    subln_g, conv_w, conv_b, w_rg_a, b_rg_a, w_rg_x, b_rg_x, rg_lambda, w_br_attn, w_br_rnn,
    w_out, norm2_g, w_peer_q, peer_sub_keys, peer_u, peer_v, mem_2, positions_2, g_ffn1_2,
    w_ffn1_gate_2, w_ffn1_up_2, w_ffn1_down_2, g_mix_2, w_in_2, g_q_2, g_k_2, sinks_2, w_dw_2,
    b_dw_2, g_conv_ln_2, b_conv_ln_2, g_mem_2, w_mem_kv_2, g_mq_2, g_mk_2, w_out_2, g_ffn2_2,
    w_ffn2_gate_2, w_ffn2_up_2, w_ffn2_down_2,
):
    x = first_block(
        x, norm1_g, w_in, b_gate, q_norm_g, k_norm_g, lambda_q1, lambda_k1, lambda_q2,
        lambda_k2, subln_g, conv_w, conv_b, w_rg_a, b_rg_a, w_rg_x, b_rg_x, rg_lambda,
        w_br_attn, w_br_rnn, w_out, norm2_g, w_peer_q, peer_sub_keys, peer_u, peer_v,
    )
    return second_block(
        x, mem_2, positions_2, g_ffn1_2, w_ffn1_gate_2, w_ffn1_up_2, w_ffn1_down_2, g_mix_2,
        w_in_2, g_q_2, g_k_2, sinks_2, w_dw_2, b_dw_2, g_conv_ln_2, b_conv_ln_2, g_mem_2,
        w_mem_kv_2, g_mq_2, g_mk_2, w_out_2, g_ffn2_2, w_ffn2_gate_2, w_ffn2_up_2,
        w_ffn2_down_2,
    )


_drawn_inputs = setup_inputs


def setup_inputs(seed=0):
    import zlib

    import numpy as np

    out = dict(_drawn_inputs(seed))
    spreads = {}
    factors = {'b_gate': 4.836,
     'q_norm_g': 3.118,
     'k_norm_g': 2.879,
     'lambda_k2': 5.692,
     'subln_g': 2.781,
     'b_rg_a': 8.0,
     'b_rg_x': 8.0,
     'g_ffn1_2': 2.948,
     'g_mix_2': 3.229,
     'g_q_2': 8.0,
     'g_k_2': 8.0,
     'sinks_2': 200.0,
     'b_dw_2': 17.972,
     'g_conv_ln_2': 17.658,
     'b_conv_ln_2': 44.163,
     'g_mem_2': 8.0,
     'g_mq_2': 8.0,
     'g_mk_2': 8.0,
     'g_ffn2_2': 3.291}
    for name, (base, spread) in spreads.items():
        noise = np.random.default_rng([zlib.crc32(name.encode()), seed]).standard_normal(out[name].shape)
        drawn = base * np.exp(spread * noise) if base else spread * noise
        out[name] = jnp.asarray(drawn.astype(out[name].dtype))
    for name, factor in factors.items():
        out[name] = (out[name] * factor).astype(out[name].dtype)
    return out
```

```python
from contextlib import ExitStack

import concourse.bass as bass
from concourse import mybir

F32 = mybir.dt.float32
F32R = mybir.dt.float32r
BF16 = mybir.dt.bfloat16
U32 = mybir.dt.uint32
I32 = mybir.dt.int32
ALU = mybir.AluOpType
ACT = mybir.ActivationFunctionType
AX_X = mybir.AxisListType.X

T = 512
D = 1024
EPS = 1e-6
LAM_INIT = 0.2
INV_FREQ = [1.0, 0.1939227432012558, 0.03760603070259094, 0.007292664609849453,
            0.0014142135623842478, 0.00027424818836152554, 5.3182957344688475e-05,
            1.0313385246263351e-05]

PCOLS = {}


def _cols():
    at = 0
    for name, n in (("norm1_g", 8), ("b_gate", 16), ("q_norm_g", 1), ("k_norm_g", 1), ("subln_g", 1),
                    ("conv_w", 40), ("conv_b", 10), ("b_rg_a", 10), ("b_rg_x", 10), ("rg_lambda", 10),
                    ("norm2_g", 8), ("g_ffn1_2", 8), ("g_mix_2", 8), ("g_q_2", 1), ("g_k_2", 1),
                    ("sinks_2", 8), ("w_dw_2", 62), ("b_dw_2", 2), ("g_conv_ln_2", 2),
                    ("b_conv_ln_2", 2), ("g_mem_2", 8), ("g_mq_2", 1), ("g_mk_2", 1), ("g_ffn2_2", 8)):
        PCOLS[name] = at
        at += n
    return at


NP = _cols()
C_ID, C_ONE, C_BLK, C_IOTA, C_PERM, C_MASK2, C_MASK1, C_INVF, C_EPS, C_EPS2, C_HPI, NC_ = (
    0, 128, 256, 384, 512, 640, 896, 960, 961, 962, 963, 964)

FG = [(0, 8), (8, 8), (16, 6)]


def unit_order():
    u = []
    for c in range(10):
        u += [("w_in", 24 + c, 1024), ("w_in", 34 + c, 1024), ("w_rg", c, 256)]
    for m in range(8):
        u += [("w_in", 52 + m, 1024), ("w_brr", 2 * m, 640), ("w_brr", 2 * m + 1, 640)]
    for h in range(8):
        u += [("w_in", h, 1024), ("w_in", 8 + h, 1024), ("w_in", 16 + h, 1024)]
    for m in range(8):
        u += [("w_in", 44 + m, 1024), ("w_bra", m, 1024)]
    u += [("w_out", m, 1024) for m in range(8)]
    U = [("pu", i, 1024) for i in range(128)]
    for j in range(16):
        u += [("w_pq", j, 1024), U.pop(0), U.pop(0), ("sk", j, 128), U.pop(0)]
        if j % 2:
            u += [U.pop(0) for _ in range(4)]
    u += U
    for g in range(16):
        for half in range(2):
            u += [("pv", (g * 2 + half) * 4 + p, 1024) for p in range(4)]
    for f in ("1", "2"):
        if f == "2":
            u += [("w_mkv", c, 1024) for c in range(4)]
            u += [("w_in2", 4, 1024), ("w_in2", 5, 1024)]
            u += [("w_in2", c, 1024) for c in (6, 8, 7, 9)]
            u += [("w_in2", c, 1024) for c in (0, 1, 2, 3, 10, 11)]
            u += [("w_out2", m, 1024) for m in range(8)]
        for gi in range(4):
            if gi < 3:
                for i in range(FG[gi][0], sum(FG[gi])):
                    u += [("wg" + f, i, 1024), ("wu" + f, i, 1024)]
            if gi > 0:
                u += [("wd" + f, (gi - 1) * 8 + m, FG[gi - 1][1] * 128) for m in range(8)]
    return u


class Queue:

    def __init__(self, sem):
        self.sem, self.items, self.n, self.seen = sem, [], 0, {}

    def wait(self, toks):
        for t in toks:
            if t is None:
                continue
            sem, v = t
            if self.seen.get(id(sem), 0) < v:
                self.seen[id(sem)] = v
                self.items.append((0, sem, v))

    def put(self, f, w=(), inc=True):
        self.wait(w)
        self.items.append((1, f, inc))
        if inc:
            self.n += 1
            return (self.sem, self.n)
        return None

    def emit(self, eng):
        for kind, a, b in self.items:
            if kind == 0:
                eng.wait_ge(a, b)
            elif kind == 2:
                a(eng).then_inc(b, 16)
            elif b:
                a(eng).then_inc(self.sem, 1)
            else:
                a(eng)


class Vec(Queue):
    def tt(self, out, a, b, op, w=()):
        return self.put(lambda e: e.tensor_tensor(out, a, b, op), w)

    def ts(self, out, a, s1, s2, op0, op1=None, w=()):
        if op1 is None:
            return self.put(lambda e: e.tensor_scalar(out, a, s1, None, op0), w)
        return self.put(lambda e: e.tensor_scalar(out, a, s1, s2, op0, op1), w)

    def stt(self, out, a, s, b, op0, op1, w=()):
        return self.put(lambda e: e.scalar_tensor_tensor(out=out, in0=a, scalar=s, in1=b, op0=op0, op1=op1), w)

    def recip(self, out, a, w=()):
        return self.put(lambda e: e.reciprocal(out, a), w)

    def copy(self, out, a, w=()):
        return self.put(lambda e: e.tensor_copy(out, a), w)

    def red(self, out, a, op, w=()):
        return self.put(lambda e: e.tensor_reduce(out, a, AX_X, op), w)

    def max8(self, out, a, w=()):
        return self.put(lambda e: e.max(out, a), w)

    def idx8(self, out, m, a, w=()):
        return self.put(lambda e: e.max_index(out, m, a), w)

    def rep8(self, out, m, a, w=()):
        return self.put(lambda e: e.match_replace(out, m, a, -3.0e38), w)

    def scan(self, out, a, b, w=()):
        return self.put(lambda e: e.tensor_tensor_scan(out, a, b, 0.0, ALU.mult, ALU.add), w)

    def fill(self, out, v, w=()):
        return self.put(lambda e: e.memset(out, v), w)


class Act(Queue):
    def act(self, out, a, func, w=(), scale=1.0, bias=None, acc=None):
        if bias is None:
            if acc is None:
                return self.put(lambda e: e.activation(out, a, func, scale=scale), w)
            return self.put(lambda e: e.activation(out, a, func, scale=scale, accum_out=acc), w)
        if acc is None:
            return self.put(lambda e: e.activation(out, a, func, bias=bias, scale=scale), w)
        return self.put(lambda e: e.activation(out, a, func, bias=bias, scale=scale, accum_out=acc), w)

    def copy(self, out, a, w=()):
        return self.put(lambda e: e.activation(out, a, ACT.Copy), w)


class Ten(Queue):
    def mm(self, out, l, r, start, stop, w=(), inc=False):
        return self.put(lambda e: e.matmul(out, l, r, start=start, stop=stop, skip_group_check=True), w, inc)

    def mm3(self, out, lh, ll, rh, rl, start, stop, w=(), inc=False):
        self.mm(out, lh, rh, start, False, w)
        self.mm(out, lh, rl, False, False)
        return self.mm(out, ll, rh, False, stop, (), inc)

    def tr(self, out, a, ident, w=(), inc=False):
        return self.put(lambda e: e.transpose(out, a, ident), w, inc)


class Sync(Queue):
    def dma(self, out, a, sem, w=()):
        self.wait(w)
        self.items.append((2, lambda e: e.dma_start(out, a), sem[0]))
        sem[1] += 16
        return (sem[0], sem[1])


class Slot:
    def __init__(self, ap, sem=None):
        self.ap, self.free, self.held, self.sem = ap, (), False, sem

    def give(self, *toks):
        assert self.held
        self.held, self.free = False, toks


class Slots:

    def __init__(self, slots):
        self.slots, self.i = slots, 0

    def take(self):
        for _ in range(len(self.slots)):
            s = self.slots[self.i % len(self.slots)]
            self.i += 1
            if not s.held:
                s.held = True
                return s
        raise AssertionError("no free slot")


def f(ap):
    return ap.bitcast(F32)


def build(nc, a, out, stop_after=None, dbg=None):
    with ExitStack() as ctx:
        nsem = [0]

        def sem():
            nsem[0] += 1
            return ctx.enter_context(nc.semaphore(f"s{nsem[0]}"))

        base = 16512
        pos = [base]

        def at(name, cols, dt, offset=None, size=4):
            off = pos[0] if offset is None else offset
            t = nc.alloc_sbuf_tensor_at(name, [128, cols], dt, offset=off)
            if offset is None:
                pos[0] += (cols * size + 31) // 32 * 32
            return t, off

        NRAW, NW = 5, 5
        raw_t, _ = at("raw", NRAW * 1024, F32)
        whl_t, _ = at("whl", NW * 2048, F32R)
        X_t, _ = at("X", 4096, F32)
        H_t, h_off = at("H", 8192, F32R)
        GA_t, _ = at("GA", 8192, F32, offset=h_off)
        S_t, s_off = at("S", 16384, F32R)
        ST_t, _ = at("ST", 16384, F32, offset=s_off)
        scr_t, _ = at("scr", 10 * 512, F32)
        pad_t, _ = at("pad", 2 * 544, F32)
        cst_t, _ = at("cst", NC_, F32)
        prm_t, _ = at("prm", NP, F32)
        cos_t, _ = at("rope", 1024, F32)
        idb_t, _ = at("idb", 128, BF16, size=2)
        m2b_t, _ = at("m2b", 256, BF16, size=2)
        m1b_t, _ = at("m1b", 64, BF16, size=2)
        sm_t, _ = at("sm", 256, F32)
        su_t, _ = at("su", 256, U32)
        assert pos[0] <= nc.sbuf_usable_end
        pb = [ctx.enter_context(nc.psum_tensor(f"pb{i}", [128, 512], F32)) for i in range(8)]
        gd = nc.dram_tensor("gd", [128, 128, 512], F32).ap()
        ad = nc.dram_tensor("ad", [128, 128, 512], F32).ap()

        V, A, P, G, S = Vec(sem()), Act(sem()), Ten(sem()), Vec(sem()), Sync(sem())

        def cst(c, n):
            return cst_t[:, c:c + n]

        def prm(name, i=0, n=1):
            return prm_t[:, PCOLS[name] + i:PCOLS[name] + i + n]

        ident, ones, blk, iota = cst(C_ID, 128), cst(C_ONE, 128), cst(C_BLK, 128), cst(C_IOTA, 128)
        perm, invf, eps, eps2, hpi = cst(C_PERM, 128), cst(C_INVF, 1), cst(C_EPS, 1), cst(C_EPS2, 1), cst(C_HPI, 1)
        X = [X_t[:, 512 * k:512 * k + 512] for k in range(8)]
        Hh = [H_t[:, 512 * k:512 * k + 512] for k in range(8)]
        Hl = [H_t[:, 4096 + 512 * k:4096 + 512 * k + 512] for k in range(8)]
        scr = Slots([Slot(scr_t[:, 512 * i:512 * i + 512], [sem(), 0]) for i in range(10)])
        bank = [Slot(pb[i][:, :]) for i in range(8)]

        units = unit_order()
        wsem = [[sem(), 0] for _ in range(NRAW)]
        raw_free = [() for _ in range(NRAW)]
        part_free = [() for _ in range(NW)]
        st = {"dma": 0, "split": 0, "get": 0}
        landed, parted = {}, {}

        def w_load():
            j = st["dma"]
            if j >= len(units):
                return
            name, i, n = units[j]
            r = j % NRAW
            landed[j] = S.dma(raw_t[:, r * 1024:r * 1024 + n], a[name][i, :, 0:n], wsem[r], w=raw_free[r])
            st["dma"] += 1

        def w_split():
            j = st["split"]
            if j >= len(units):
                return
            n = units[j][2]
            r, q = j % NRAW, j % NW
            src = raw_t[:, r * 1024:r * 1024 + n]
            hi = whl_t[:, q * 2048:q * 2048 + n]
            lo = whl_t[:, q * 2048 + 1024:q * 2048 + 1024 + n]
            assert part_free[q] is not None
            t1 = A.copy(hi, src, w=(landed[j],) + part_free[q])
            t2 = V.tt(lo, src, f(hi), ALU.subtract, w=(t1,))
            parted[j] = (hi, lo, t2)
            part_free[q] = None
            raw_free[r] = (t2,)
            st["split"] += 1
            w_load()

        def w_get(name, i):
            j = st["get"]
            assert units[j][:2] == (name, i), (units[j], name, i)
            while st["split"] < min(j + NW, len(units)):
                w_split()
            st["get"] += 1
            hi, lo, t = parted.pop(j)
            return hi, lo, t, j

        def w_done(j, tok):
            part_free[j % NW] = (tok,)

        c_sem, p_sem, x_sem = [sem(), 0], [sem(), 0], [sem(), 0]
        x_in = S.dma(X_t[:, :].rearrange("p (k t) -> p k t", k=8), a["x"], x_sem)
        c_in = S.dma(cst_t[:, :], a["cst"], c_sem)
        p_in = S.dma(prm_t[:, :], a["prm"], p_sem)
        for _ in range(NRAW):
            w_load()
        lam_s = scr.take()
        lam_in = S.dma(lam_s.ap[:, 0:256], a["lambdas"], lam_s.sem)
        V.copy(idb_t[:, :], ident, w=(c_in, p_in))
        V.copy(m2b_t[:, :], cst(C_MASK2, 256))
        masks = V.copy(m1b_t[:, :], cst(C_MASK1, 64))
        for e in (A, P, G):
            e.wait((c_in, p_in))

        def sums(chunks, toks, lhs, b, n):
            last = None
            for k, c in enumerate(chunks):
                s = scr.take()
                t = A.act(s.ap[:, 0:n], c, ACT.Square, w=(toks[k],) + tuple(s.free))
                last = P.mm(b.ap[:, 0:n], lhs, s.ap[:, 0:n], k == 0, k == len(chunks) - 1,
                            w=(t,) + (tuple(b.free) if k == 0 else ()), inc=True)
                s.give(last)
            return last

        def rstd(b, n, width, tok, gain=1.0, bias=None):
            r = scr.take()
            t = A.act(r.ap[:, 0:n], b.ap[:, 0:n], ACT.Sqrt, w=(tok,) + tuple(r.free),
                      scale=gain / width, bias=eps if bias is None else bias)
            b.give(t)
            t = V.recip(r.ap[:, 0:n], r.ap[:, 0:n], w=(t,))
            return r, t

        def norm(chunks, toks, gains, hi, lo, n, free=()):
            b = bank[7]
            assert not b.held
            b.held = True
            t = sums(chunks, toks, ones, b, n)
            r, t = rstd(b, n, D, t)
            res, prev = [], None
            for k in range(len(chunks) + 1):
                if k < len(chunks):
                    s = scr.take()
                    t1 = V.stt(s.ap[:, 0:n], chunks[k], gains[k], r.ap[:, 0:n], ALU.mult, ALU.mult,
                               w=(t,) + tuple(s.free))
                    t2 = A.copy(hi[k], s.ap[:, 0:n], w=(t1,) + tuple(free))
                if prev is not None:
                    s0, k0, h0 = prev
                    t3 = V.tt(lo[k0], s0.ap[:, 0:n], f(hi[k0]), ALU.subtract, w=(h0,) + tuple(free))
                    s0.give(t3)
                    res.append(t3)
                prev = (s, k, t2) if k < len(chunks) else None
            r.give(res[-1])
            return res

        def linear(name, i, b, hh, hl, toks, n=T, w=(), start=True, stop=True, kk=8, take=True):
            hi, lo, t, j = w_get(name, i)
            if take:
                assert not b.held
                b.held = True
                w = tuple(w) + tuple(b.free)
            for k in range(kk):
                last = P.mm3(b.ap[:, 0:n], hi[:, 128 * k:128 * k + 128], lo[:, 128 * k:128 * k + 128],
                             hh[k], hl[k], start and k == 0, stop and k == kk - 1,
                             w=((t,) + tuple(w) if k == 0 else ()) + (toks[k],), inc=k == kk - 1)
            w_done(j, last)
            return last

        def parts(src, hi, lo, w=(), free=()):
            t = A.copy(hi, src, w=tuple(w) + tuple(free))
            return V.tt(lo, src, f(hi), ALU.subtract, w=(t,) + tuple(w))

        lm = lam_s.ap
        t = V.tt(sm_t[:, 128:192], lm[:, 0:64], lm[:, 64:128], ALU.mult, w=(lam_in,))
        t = V.tt(sm_t[:, 192:256], lm[:, 128:192], lm[:, 192:256], ALU.mult)
        lam_s.give(t)
        t = V.red(sm_t[:, 0:1], sm_t[:, 128:192], ALU.add, w=(t,))
        t = V.red(sm_t[:, 1:2], sm_t[:, 192:256], ALU.add)
        t = A.act(sm_t[:, 2:4], sm_t[:, 0:2], ACT.Exp, w=(t,))
        t = V.tt(sm_t[:, 4:5], sm_t[:, 2:3], sm_t[:, 3:4], ALU.subtract, w=(t,))
        neglam = sm_t[:, 5:6]
        t = V.ts(neglam, sm_t[:, 4:5], LAM_INIT, -1.0, ALU.add, ALU.mult, w=(t,))
        lam = prm("rg_lambda", 0, 10)
        q = [sm_t[:, 16 + 10 * i:26 + 10 * i] for i in range(6)]
        nsp, nsp2 = q[4], q[5]
        t = V.ts(q[0], lam, -1.0, None, ALU.mult, w=(p_in,))
        t = V.tt(q[1], lam, q[0], ALU.min, w=(t,))
        t = A.act(q[1], q[1], ACT.Exp, w=(t,))
        t = V.ts(q[2], q[1], 2.0, None, ALU.add, w=(t,))
        t = V.recip(q[2], q[2], w=(t,))
        t = V.tt(q[1], q[1], q[2], ALU.mult, w=(t,))
        t = V.tt(q[2], q[1], q[1], ALU.mult, w=(t,))
        t = V.ts(q[3], q[2], 1.0 / 19, 1.0 / 17, ALU.mult, ALU.add, w=(t,))
        for d in (15, 13, 11, 9, 7, 5, 3, 1):
            t = V.tt(q[3], q[3], q[2], ALU.mult, w=(t,))
            t = V.ts(q[3], q[3], 1.0 / d, None, ALU.add, w=(t,))
        t = V.stt(q[3], q[3], 2.0, q[1], ALU.mult, ALU.mult, w=(t,))
        t = V.stt(q[3], q[0], 0.0, q[3], ALU.max, ALU.add, w=(t,))
        sp_tok = V.ts(nsp, q[3], -8.0, None, ALU.mult, w=(t,))
        A.wait((sp_tok,))

        x_tok = [x_in] * 8
        pad = [pad_t[:, 544 * i:544 * i + 544] for i in range(2)]
        pad0 = [V.fill(pad[i][:, 0:32], 0.0) for i in range(2)]
        pad_free = [(), ()]

        h1 = norm(X, x_tok, [prm("norm1_g", k) for k in range(8)], Hh, Hl, T)

        def rope_tables():
            pos_s = scr.take()
            pos_in = S.dma(pos_s.ap.bitcast(I32), a["pos"], pos_s.sem, w=tuple(pos_s.free))
            s = [scr.take() for _ in range(3)]
            ang, n, r = s[0].ap, s[1].ap, s[2].ap
            t = V.copy(n, pos_s.ap.bitcast(I32), w=(pos_in,) + tuple(s[1].free))
            pos_s.give(t)
            t = V.ts(ang, n, invf, None, ALU.mult, w=(t,) + tuple(s[0].free))
            t = V.ts(n, ang, 0.15915494309189535, None, ALU.mult, w=(t,))
            t = V.ts(n, n, 12582912.0, None, ALU.add, w=(t,))
            t = V.ts(n, n, -12582912.0, None, ALU.add, w=(t,))
            for c in (6.28125, 0.0019350051879882812, 3.0199e-07):
                t = V.stt(ang, n, -c, ang, ALU.mult, ALU.add, w=(t,))
            t = V.ts(ang, ang, 3.1415925, -3.1415925, ALU.min, ALU.max, w=(t,))
            cs, sn = cos_t[:, 0:512], cos_t[:, 512:1024]
            t1 = A.act(sn, ang, ACT.Sin, w=(t,))
            t = V.stt(r, ang, -1.0, ang, ALU.mult, ALU.max, w=(t,) + tuple(s[2].free))
            t = A.act(cs, r, ACT.Sin, w=(t,), scale=-1.0, bias=hpi)
            for x in s:
                x.give(t)
            return t

        rh = [S_t[:, 512 * c:512 * c + 512] for c in range(10)]
        rl = [S_t[:, 5120 + 512 * c:5120 + 512 * c + 512] for c in range(10)]
        cvh = [S_t[:, 10240 + 512 * i:10752 + 512 * i] for i in range(2)]
        cvl = [S_t[:, 11264 + 512 * i:11776 + 512 * i] for i in range(2)]
        r_tok = []
        cv_free = [(), ()]

        def rnn_chunk(c):
            i = c % 2
            b = bank[i]
            t = linear("w_in", 24 + c, b, Hh, Hl, h1)
            t = A.copy(pad[i][:, 32:544], b.ap, w=(t,) + tuple(pad_free[i]))
            b.give(t)
            cv = scr.take()
            wv = [prm("conv_w", 4 * c + j) for j in range(4)]
            t = V.ts(cv.ap, pad[i][:, 32:544], wv[3], prm("conv_b", c), ALU.mult, ALU.add,
                     w=(t,) + tuple(cv.free))
            for j in (2, 1, 0):
                t = V.stt(cv.ap, pad[i][:, 29 + j:541 + j], wv[j], cv.ap, ALU.mult, ALU.add, w=(t,))
            pad_free[i] = (t,)
            pt = parts(cv.ap, cvh[i], cvl[i], w=(t,), free=cv_free[i])
            by = bank[2 + i]
            t = linear("w_in", 34 + c, by, Hh, Hl, h1)
            gy = scr.take()
            gt = A.act(gy.ap, by.ap, ACT.Gelu_apprx_tanh, w=(t,) + tuple(gy.free))
            by.give(gt)
            hi, lo, wt, j = w_get("w_rg", c)
            br, bx = bank[4], bank[5]
            br.held = bx.held = True
            tr = P.mm3(br.ap, hi[:, 0:128], lo[:, 0:128], cvh[i], cvl[i], True, True,
                       w=(wt, pt) + tuple(br.free), inc=True)
            tx = P.mm3(bx.ap, hi[:, 128:256], lo[:, 128:256], cvh[i], cvl[i], True, True,
                       w=tuple(bx.free), inc=True)
            w_done(j, tx)
            cv_free[i] = (tx,)
            r, g, m = scr.take(), scr.take(), scr.take()
            t = A.act(r.ap, br.ap, ACT.Sigmoid, w=(tr,) + tuple(r.free), bias=prm("b_rg_a", c))
            br.give(t)
            t2 = A.act(g.ap, bx.ap, ACT.Sigmoid, w=(tx,) + tuple(g.free), bias=prm("b_rg_x", c))
            bx.give(t2)
            gx = V.tt(g.ap, g.ap, cv.ap, ALU.mult, w=(t2,))
            t = A.act(m.ap, r.ap, ACT.Tanh, w=(t,) + tuple(m.free), scale=nsp[:, c:c + 1])
            ta = A.act(r.ap, r.ap, ACT.Exp, w=(t,), scale=nsp[:, c:c + 1])
            t = A.act(cv.ap, r.ap, ACT.Square, w=(ta, gx, pt))
            t = V.stt(m.ap, cv.ap, 1.0, m.ap, ALU.add, ALU.mult, w=(t,))
            t = A.act(m.ap, m.ap, ACT.Sqrt, w=(t,), scale=-1.0)
            t = V.tt(g.ap, g.ap, m.ap, ALU.mult, w=(t,))
            t = V.scan(cv.ap, r.ap, g.ap, w=(t,))
            r.give(t)
            g.give(t)
            m.give(t)
            t = V.tt(gy.ap, gy.ap, cv.ap, ALU.mult, w=(t, gt))
            cv.give(t)
            t = parts(gy.ap, rh[c], rl[c], w=(t,))
            gy.give(t)
            r_tok.append(t)

        for c in range(10):
            rnn_chunk(c)

        m_tok = []
        for m in range(8):
            bg, bo = bank[m % 2], bank[2 + m % 2]
            t = linear("w_in", 52 + m, bg, Hh, Hl, h1)
            s = scr.take()
            tg = A.act(s.ap, bg.ap, ACT.Sigmoid, w=(t,) + tuple(s.free), bias=prm("b_gate", 8 + m))
            bg.give(tg)
            linear("w_brr", 2 * m, bo, rh[0:5], rl[0:5], r_tok[0:5], kk=5, stop=False)
            t = linear("w_brr", 2 * m + 1, bo, rh[5:10], rl[5:10], r_tok[5:10], kk=5, start=False, take=False)
            rn_last = t
            t = V.tt(X[m], bo.ap, s.ap, ALU.mult, w=(t, tg, h1[m]))
            bo.give(t)
            s.give(t)
            m_tok.append(t)

        def region(o, n):
            return S_t[:, o:o + n]

        oh = [region(512 * h, 512) for h in range(8)]
        ol = [region(4096 + 512 * h, 512) for h in range(8)]
        qk = [[region(8192 + 2048 * i + 512 * j, 512) for j in range(4)] for i in range(2)]
        vv = [[region(12288 + 1024 * i + 512 * j, 512) for j in range(2)] for i in range(2)]
        dts = Slots([Slot([region(14336 + 1024 * i + 512 * j, 512) for j in range(2)]) for i in range(2)])
        for s in dts.slots:
            s.free = (rn_last,)
        qk_free = [(rn_last,), (rn_last,)]
        vv_free = [(rn_last,), (rn_last,)]

        def head_norm(b, t, gain, lhs, width, hi, lo, free):
            n7 = bank[7]
            n7.held = True
            t1 = sums([b.ap], [t], lhs, n7, T)
            r, t1 = rstd(n7, T, width, t1)
            t2 = V.stt(r.ap, b.ap, gain, r.ap, ALU.mult, ALU.mult, w=(t1,))
            b.give(t2)
            t3 = parts(r.ap, hi, lo, w=(t2,), free=free)
            r.give(t3)
            return t3

        def to_rows(b, t, hi, lo, free, n=4):
            s = scr.take()
            w = 128 * n
            t = A.copy(s.ap[:, 0:w], b.ap[:, 0:w], w=(t,) + tuple(s.free))
            b.give(t)
            n7 = bank[7]
            n7.held = True
            for k in range(n):
                tt = P.tr(n7.ap[:, 128 * k:128 * k + 128], s.ap[:, 128 * k:128 * k + 128], ident,
                          w=(t,) + (tuple(n7.free) if k == 0 else ()), inc=k == n - 1)
            s.give(tt)
            t = parts(n7.ap[:, 0:w], hi, lo, w=(tt,), free=free)
            n7.give(t)
            return t

        def proj(h):
            i = h % 2
            q_h, q_l, k_h, k_l = qk[i]
            b = bank[0]
            t = linear("w_in", h, b, Hh, Hl, h1)
            yield
            tq = head_norm(b, t, prm("q_norm_g"), blk, 64, q_h, q_l, qk_free[i])
            b = bank[1]
            t = linear("w_in", 8 + h, b, Hh, Hl, h1)
            yield
            tk = head_norm(b, t, prm("k_norm_g"), blk, 64, k_h, k_l, qk_free[i])
            b = bank[0]
            t = linear("w_in", 16 + h, b, Hh, Hl, h1)
            yield
            tv = to_rows(b, t, vv[i][0], vv[i][1], vv_free[i])
            ready[h] = (tq, tk, tv)

        ready = {}
        o_tok = [None] * 8
        sbank = Slots([Slot([bank[2], bank[3]]), Slot([bank[4], bank[5]])])
        for s in sbank.slots:
            s.free = tuple(t for b in s.ap for t in b.free)

        def soft(sb, tok, n, scale, small, sink=None):
            mx = sm_t[:, small:small + 2]
            nm, sm, rc = (sm_t[:, small + 2 * i:small + 2 * i + 2] for i in (1, 2, 3))
            V.red(mx[:, 0:1], sb.ap[0].ap[:, 0:n], ALU.max, w=(tok,) + sm_free[small])
            t = V.red(mx[:, 1:2], sb.ap[1].ap[:, 0:n], ALU.max)
            if sink is None:
                t = V.ts(nm, mx, -scale, None, ALU.mult, w=(t,))
            else:
                t = V.ts(mx, mx, scale, None, ALU.mult, w=(t,))
                t = V.tt(mx, mx, sink, ALU.max, w=(t,))
                t = V.ts(nm, mx, -1.0, None, ALU.mult, w=(t,))
            ps, ts = [], []
            for c in range(2):
                p = scr.take()
                te = A.act(p.ap[:, 0:n], sb.ap[c].ap[:, 0:n], ACT.Exp, w=(t,) + tuple(p.free),
                           scale=scale, bias=nm[:, c:c + 1], acc=sm[:, c:c + 1])
                ps.append(p)
                ts.append(te)
            sb.give(te)
            if sink is not None:
                sk_ = sm_t[:, small + 8:small + 10]
                t = V.tt(sk_, sink, nm, ALU.add, w=(t,))
                t = A.act(sk_, sk_, ACT.Exp, w=(t,))
                t = V.tt(sm, sm, sk_, ALU.add, w=(t, te))
                t = V.recip(rc, sm, w=(t,))
            else:
                t = V.recip(rc, sm, w=(te,))
            return ps, rc, t

        sm_free = {80: (), 96: (), 112: (), 64: ()}

        def turned(dd, tok, n, T6):
            T6.held = True
            for k in range(n):
                t = P.tr(T6.ap[:, 128 * k:128 * k + 128], dd[:, 128 * k:128 * k + 128], ident,
                         w=(tok,) + (tuple(T6.free) if k == 0 else ()), inc=k == n - 1)
            d = dts.take()
            t2 = parts(T6.ap[:, 0:128 * n], d.ap[0][:, 0:128 * n], d.ap[1][:, 0:128 * n], w=(t,),
                       free=tuple(d.free))
            T6.give(t2)
            return d, t, t2

        def attend(h):
            i = h % 2
            tq, tk, tv = ready[h]
            q_h, q_l, k_h, k_l = qk[i]
            ob = bank[1]
            last_s = None
            for qb in range(4):
                n = 128 * (qb + 1)
                sb = sbank.take()
                for c in range(2):
                    b, r = sb.ap[c].ap, slice(64 * c, 64 * c + 64)
                    P.mm3(b[:, 0:n], q_h[r, 128 * qb:128 * qb + 128], q_l[r, 128 * qb:128 * qb + 128],
                          k_h[r, 0:n], k_l[r, 0:n], True, False, w=(tq, tk) + tuple(sb.free))
                    t = P.mm(b[:, n - 64:n], idb_t[:, :], m1b_t[:, :], False, True, w=(masks,), inc=True)
                last_s = t
                small = 80 if qb % 2 else 64
                ps, rc, t = soft(sb, t, n, 0.125, small)
                t = V.tt(rc[:, 1:2], rc[:, 1:2], neglam, ALU.mult, w=(t,))
                t = V.ts(ps[1].ap[:, 0:n], ps[1].ap[:, 0:n], rc[:, 1:2], None, ALU.mult, w=(t,))
                t = V.stt(ps[0].ap[:, 0:n], ps[0].ap[:, 0:n], rc[:, 0:1], ps[1].ap[:, 0:n],
                          ALU.mult, ALU.add, w=(t,))
                ps[1].give(t)
                sm_free[small] = (t,)
                yield
                d, tp, t = turned(ps[0].ap, t, qb + 1, bank[6])
                ps[0].give(tp)
                yield
                if qb == 0:
                    while ob.held:
                        yield
                    ob.held = True
                for k in range(qb + 1):
                    vs = slice(128 * k, 128 * k + 128)
                    t2 = P.mm3(ob.ap[:, 128 * qb:128 * qb + 128], vv[i][0][:, vs], vv[i][1][:, vs],
                               d.ap[0][:, vs], d.ap[1][:, vs], k == 0, k == qb,
                               w=(t, tv) + (tuple(ob.free) if qb == 0 and k == 0 else ()), inc=k == qb)
                d.give(t2)
            qk_free[i] = (last_s,)
            vv_free[i] = (t2,)
            n7 = bank[7]
            n7.held = True
            t1 = sums([ob.ap], [t2], ones, n7, T)
            r, t1 = rstd(n7, T, 128, t1, gain=1.0 / 0.64, bias=eps2)
            t2 = V.stt(r.ap, ob.ap, prm("subln_g"), r.ap, ALU.mult, ALU.mult, w=(t1,))
            ob.give(t2)
            t3 = parts(r.ap, oh[h], ol[h], w=(t2,), free=(rn_last,))
            r.give(t3)
            o_tok[h] = t3

        def together(fore, back):
            fore, back = list(fore), list(back)
            while fore or back:
                for q in (fore, back):
                    if q:
                        try:
                            next(q[0])
                        except StopIteration:
                            q.pop(0)

        for _ in proj(0):
            pass
        for h in range(8):
            together([attend(h)], [proj(h + 1)] if h < 7 else [])

        mh, ml = ([region(8192 + 512 * m, 512) for m in range(8)],
                              [region(12288 + 512 * m, 512) for m in range(8)])
        g_tok = []
        for m in range(8):
            bg, bo = bank[m % 2], bank[2 + m % 2]
            bo.free = tuple(bo.free) + tuple(sbank.slots[0].free)
            t = linear("w_in", 44 + m, bg, Hh, Hl, h1)
            s = scr.take()
            tg = A.act(s.ap, bg.ap, ACT.Sigmoid, w=(t,) + tuple(s.free), bias=prm("b_gate", m))
            bg.give(tg)
            t = linear("w_bra", m, bo, oh, ol, o_tok)
            last_bra = t
            t = V.tt(s.ap, bo.ap, s.ap, ALU.mult, w=(t, tg))
            bo.give(t)
            t = V.tt(s.ap, s.ap, X[m], ALU.add, w=(t, m_tok[m]))
            t = parts(s.ap, mh[m], ml[m], w=(t,), free=tuple(vv_free[0]) + tuple(vv_free[1]) + tuple(qk_free[1]))
            s.give(t)
            g_tok.append(t)
        x_back = S.dma(X_t[:, :].rearrange("p (k t) -> p k t", k=8), a["x"], x_sem, w=(g_tok[7],))
        x1 = []
        for m in range(8):
            b = bank[m % 2]
            t = linear("w_out", m, b, mh, ml, g_tok)
            t2 = V.tt(X[m], X[m], b.ap, ALU.add, w=(t, x_back))
            b.give(t2)
            x1.append(t2)
        last_out = t

        def finish(toks):
            tt = S.dma(out.rearrange("(k p) t -> p k t", p=128),
                       X_t[:, :].rearrange("p (k t) -> p k t", k=8), x_sem, w=tuple(toks))
            S.wait((tt,))

        def peer():
            h2 = norm(X, x1, [prm("norm2_g", k) for k in range(8)], Hh, Hl, T)
            ST = ST_t[:, :]
            spill = []
            ub = Slots([bank[0], bank[1]])
            G1 = Slots([bank[4], bank[5]])

            def u_chunks():
                for i in range(128):
                    b = ub.take()
                    b.held = False
                    t = linear("pu", i, b, Hh, Hl, h2)
                    s = scr.take()
                    t = A.act(s.ap, b.ap, ACT.Gelu_apprx_tanh, w=(t,) + tuple(s.free))
                    b.give(t)
                    tt = S.dma(ad[i, :, :], s.ap, s.sem, w=(t,))
                    s.give(tt)
                    spill.append(tt)
                    yield

            qh, ql = [region(15360, 512), region(14336, 512)], [region(15872, 512), region(14848, 512)]
            q_free = [(last_out,), (last_out,)]
            vals = sm_t[:, 0:128].rearrange("p (c b k) -> p c b k", c=2, b=4)
            idxf = sm_t[:, 128:256].rearrange("p (c b k) -> p c b k", c=2, b=4)
            idxu = su_t[:, 0:128].rearrange("p (c b k) -> p c b k", c=2, b=4)
            posu = su_t[:, 128:192]
            pt = su_t[:, 192:256]
            I1, I2, TS = scr.take(), scr.take(), scr.take()
            V.wait(tuple(I1.free) + tuple(I2.free) + tuple(TS.free) + (last_out,))
            v4 = {id(z): z.ap.rearrange("p (b h k) -> p b h k", b=4, h=8) for z in (I1, I2, TS)}
            cand = ST[:, 0:1024].rearrange("p (b i j) -> p b i j", b=4, i=16)
            cand2 = ST[:, 1024:2048]
            eq = ST[:, 2048:3072].rearrange("p (b k a) -> p b k a", b=4, k=16)
            sc2 = ST[:, 3072:3200]
            pf = ST[:, 3200:3264].rearrange("p (b k) -> p b k", b=4)

            def topk():
                for h in range(8):
                    for c in range(2):
                        j = 2 * h + c
                        b = bank[2]
                        t = linear("w_pq", j, b, Hh, Hl, h2)
                        t = parts(b.ap, qh[c], ql[c], w=(t,), free=q_free[c])
                        b.give(t)
                        yield
                        yield
                        hi, lo, wt, jj = w_get("sk", j)
                        b = bank[3]
                        assert not b.held
                        b.held = True
                        for tb in range(4):
                            ts = slice(128 * tb, 128 * tb + 128)
                            t1 = P.mm3(b.ap[:, ts], qh[c][:, ts], ql[c][:, ts], hi, lo, True, True,
                                       w=(t, wt) + (tuple(b.free) if tb == 0 else ()), inc=tb == 3)
                        w_done(jj, t1)
                        q_free[c] = (t1,)
                        for tb in range(4):
                            sc = b.ap[:, 128 * tb:128 * tb + 128]
                            v, ix = vals[:, c, tb, :], idxu[:, c, tb, :]
                            t = V.max8(v[:, 0:8], sc, w=(t1,))
                            t = V.idx8(ix[:, 0:8], v[:, 0:8], sc, w=(t,))
                            t = V.rep8(sc2, v[:, 0:8], sc, w=(t,))
                            t = V.max8(v[:, 8:16], sc2, w=(t,))
                            t = V.idx8(ix[:, 8:16], v[:, 8:16], sc2, w=(t,))
                        b.give(t)
                        yield
                    t = V.copy(idxf, idxu, w=(t,))
                    s1 = vals[:, 0, :, :].unsqueeze(3).to_broadcast([128, 4, 16, 16])
                    s2 = vals[:, 1, :, :].unsqueeze(2).to_broadcast([128, 4, 16, 16])
                    for tb in range(4):
                        t = V.tt(cand[:, tb], s1[:, tb], s2[:, tb], ALU.add, w=(t,))
                    for tb in range(4):
                        cf = ST[:, 256 * tb:256 * tb + 256]
                        c2 = cand2[:, 256 * tb:256 * tb + 256]
                        top = v4[id(TS)][:, tb, h, :]
                        pu = posu[:, 16 * tb:16 * tb + 16]
                        t = V.max8(top[:, 0:8], cf, w=(t,))
                        t = V.idx8(pu[:, 0:8], top[:, 0:8], cf, w=(t,))
                        t = V.rep8(c2, top[:, 0:8], cf, w=(t,))
                        t = V.max8(top[:, 8:16], c2, w=(t,))
                        t = V.idx8(pu[:, 8:16], top[:, 8:16], c2, w=(t,))
                        if tb % 2:
                            yield
                    it = iota[:, 0:16].unsqueeze(1).to_broadcast([128, 64, 16])
                    eq3 = ST[:, 2048:3072].rearrange("p (q a) -> p q a", q=64)
                    pf2 = ST[:, 3200:3264]
                    for c, (op, imm, dst) in enumerate(((ALU.logical_shift_right, 4, I1),
                                                        (ALU.bitwise_and, 15, I2))):
                        t = V.ts(pt, posu, imm, None, op, w=(t,))
                        t = V.copy(pf2, pt, w=(t,))
                        t = V.tt(eq3, it, pf2.unsqueeze(2).to_broadcast([128, 64, 16]), ALU.is_equal, w=(t,))
                        for tb in range(4):
                            t = V.tt(eq[:, tb], eq[:, tb],
                                     idxf[:, c, tb, :].unsqueeze(1).to_broadcast([128, 16, 16]),
                                     ALU.mult, w=(t,))
                        t = V.red(v4[id(dst)][:, :, h, :], eq, ALU.add, w=(t,))
                        state["t"] = t
                        yield

            state = {}

            def experts():
                for _ in topk():
                    yield
                t = state["t"]
                ts3 = TS.ap.rearrange("p (g k) -> p g k", k=16)
                mxs = sm_t[:, 0:32]
                t = V.red(mxs, ts3, ALU.max, w=(t,))
                t = V.tt(ts3, ts3, mxs.unsqueeze(2).to_broadcast([128, 32, 16]), ALU.subtract, w=(t,))
                t = A.act(TS.ap, TS.ap, ACT.Exp, w=(t,))
                t = V.red(mxs, ts3, ALU.add, w=(t,))
                t = V.recip(mxs, mxs, w=(t,))
                t = V.tt(ts3, ts3, mxs.unsqueeze(2).to_broadcast([128, 32, 16]), ALU.mult, w=(t,))
                yield
                tk = []
                for z in (I1, I2, TS):
                    b = bank[6]
                    b.held = True
                    for tb in range(4):
                        p = P.tr(b.ap[:, 128 * tb:128 * tb + 128], z.ap[:, 128 * tb:128 * tb + 128], ident,
                                 w=(t,) + (tuple(b.free) if tb == 0 else ()), inc=tb == 3)
                    t4 = V.copy(z.ap, b.ap, w=(p,))
                    b.give(t4)
                    tk.append(t4)
                    yield
                ohA = Slots([Slot(oa_t[:, 512 * i:512 * i + 512]) for i in range(2)])
                ohB = Slots([Slot(ob_t[:, 512 * i:512 * i + 512]) for i in range(2)])
                stage = ST[:, :].rearrange("p (i t) -> p i t", i=128)
                st_free = (t,)
                gsem = [sem(), 0]
                for tb in range(4):
                    for g in range(32):
                        sa, sb_ = ohA.take(), ohB.take()
                        b = G1.take()
                        for u in range(4):
                            tok = 128 * tb + 4 * g + u
                            ta = G.ts(sa.ap[:, 128 * u:128 * u + 128], iota, I1.ap[:, tok:tok + 1], None,
                                      ALU.is_equal, w=(tk[2],) + tuple(sa.free))
                            tb_ = V.ts(sb_.ap[:, 128 * u:128 * u + 128], iota, I2.ap[:, tok:tok + 1],
                                       TS.ap[:, tok:tok + 1], ALU.is_equal, ALU.mult,
                                       w=(tk[2],) + tuple(sb_.free))
                        for u in range(4):
                            us = slice(128 * u, 128 * u + 128)
                            p = P.mm(b.ap[:, us], sb_.ap[:, us], sa.ap[:, us], True, True,
                                     w=(ta, tb_) + tuple(b.free), inc=u == 3)
                        sa.give(p)
                        sb_.give(p)
                        t = A.copy(stage[:, :, 4 * g:4 * g + 4].rearrange("p i u -> p u i"),
                                   b.ap.rearrange("p (u i) -> p u i", u=4), w=(p,) + tuple(st_free))
                        b.give(t)
                        st_free = ()
                        if g % 3 == 2:
                            yield
                    st_free = (S.dma(gd[:, :, 128 * tb:128 * tb + 128].rearrange("i p t -> p i t"), stage,
                                     gsem, w=(t,)),)
                gdone.append(st_free[0])
                for z in (I1, I2, TS):
                    z.give(t)

            gdone = []
            uc = u_chunks()
            ex = experts()
            n_u = 0
            while True:
                try:
                    next(ex)
                except StopIteration:
                    break
                if next(uc, 0) != 0:
                    n_u += 1
            for _ in uc:
                pass

            h_last = P.n
            ga = Slots([Slot((GA_t[:, 2048 * i:2048 * i + 1024], GA_t[:, 2048 * i + 1024:2048 * i + 2048]),
                             [sem(), 0]) for i in range(4)])
            for s in ga.slots:
                s.free = (u_last(P),)
            S.wait(tuple(spill) + tuple(gdone))
            wac = [Slot((region(8192 * i, 4096), region(8192 * i + 4096, 4096))) for i in range(2)]
            for w_ in wac:
                w_.free = (gdone[0],)
            loads = []

            def ga_load(p):
                s = ga.take()
                S.dma(s.ap[0].rearrange("p (i t) -> p i t", i=2),
                      gd[2 * p:2 * p + 2, :, :].rearrange("i p t -> p i t"), s.sem, w=tuple(s.free))
                t = S.dma(s.ap[1].rearrange("p (i t) -> p i t", i=2),
                          ad[2 * p:2 * p + 2, :, :].rearrange("i p t -> p i t"), s.sem)
                loads.append((s, t))

            x_last = list(h2)
            toks = {}

            def weigh(g):
                w_ = wac[g % 2]
                res = []
                for p in range(4):
                    s, t = loads.pop(0)
                    t = V.tt(s.ap[1], s.ap[0], s.ap[1], ALU.mult, w=(t,))
                    t = parts(s.ap[1], w_.ap[0][:, 1024 * p:1024 * p + 1024],
                              w_.ap[1][:, 1024 * p:1024 * p + 1024], w=(t,), free=tuple(w_.free))
                    s.give(t)
                    if 4 * g + p + 4 < 64:
                        ga_load(4 * g + p + 4)
                    res.append(t)
                    yield
                toks[g] = res

            for p in range(4):
                ga_load(p)
            for _ in weigh(0):
                pass
            for g in range(16):
                nxt = weigh(g + 1) if g < 15 else iter(())
                w_ = wac[g % 2]
                for half in range(2):
                    bs = [bank[4 * half + d] for d in range(4)]
                    for b in bs:
                        assert not b.held
                        b.held = True
                    for p in range(4):
                        hi, lo, t, j = w_get("pv", (g * 2 + half) * 4 + p)
                        for i in range(2):
                            for d in range(4):
                                ws = slice(512 * i + 128 * d, 512 * i + 128 * d + 128)
                                rs = slice(1024 * p + 512 * i, 1024 * p + 512 * i + 512)
                                last = P.mm3(bs[d].ap, hi[:, ws], lo[:, ws], w_.ap[0][:, rs], w_.ap[1][:, rs],
                                             p == 0 and i == 0, p == 3 and i == 1,
                                             w=(t, toks[g][p]) + (tuple(bs[d].free) if p == 0 and i == 0 else ()),
                                             inc=p == 3 or (i == 1 and d == 3))
                                if p == 3 and i == 1:
                                    bs[d].give(last)
                        w_done(j, last)
                        next(nxt, None)
                    for d in range(4):
                        k = 4 * half + d
                        x_last[k] = V.tt(X[k], X[k], bs[d].ap, ALU.add, w=tuple(bs[d].free) + (x_last[k],))
                        bs[d].free = (x_last[k],)
                w_.free = (last,)
                for _ in nxt:
                    pass
            return x_last

        def u_last(q):
            return (q.sem, q.n)

        oa_t, ob_t = pad_t, cos_t

        def ffn(tag, gname, xt):
            s_free0 = u_last(P)
            hx = norm(X, xt, [prm(gname, k) for k in range(8)], Hh, Hl, T, free=(s_free0,))
            sl = Slots([Slot((region(1024 * i, 512), region(1024 * i + 512, 512))) for i in range(16)])
            for s in sl.slots:
                s.free = (s_free0,)
            held = {}
            gi_b, up_b = Slots([bank[0], bank[1]]), Slots([bank[2], bank[3]])

            def hidden(i):
                b = gi_b.take()
                b.held = False
                t = linear("wg" + tag, i, b, Hh, Hl, hx)
                s = scr.take()
                ts_ = A.act(s.ap, b.ap, ACT.Silu, w=(t,) + tuple(s.free))
                b.give(ts_)
                b = up_b.take()
                b.held = False
                t = linear("wu" + tag, i, b, Hh, Hl, hx)
                t = V.tt(s.ap, s.ap, b.ap, ALU.mult, w=(t, ts_))
                b.give(t)
                z = sl.take()
                t = parts(s.ap, z.ap[0], z.ap[1], w=(t,), free=tuple(z.free))
                s.give(t)
                held[i] = (z, t)

            xl = list(xt)
            down_b = Slots([bank[4], bank[5], bank[6]])
            for gi in range(4):
                if gi < 3:
                    for i in range(FG[gi][0], sum(FG[gi])):
                        hidden(i)
                if gi > 0:
                    first, n = FG[gi - 1]
                    zs = [held.pop(first + i) for i in range(n)]
                    for m in range(8):
                        b = down_b.take()
                        b.held = False
                        t = linear("wd" + tag, (gi - 1) * 8 + m, b, [z[0].ap[0] for z in zs],
                                   [z[0].ap[1] for z in zs], [z[1] for z in zs], kk=n)
                        t2 = V.stt(X[m], b.ap, 0.5, X[m], ALU.mult, ALU.add, w=(t, xl[m], hx[7]))
                        b.give(t2)
                        xl[m] = t2
                    for z in zs:
                        z[0].give(t)
            return xl

        def mixer(xt):
            p0 = u_last(P)
            rope_tok = rope_tables()
            for i in range(2):
                pad_free[i] = (V.fill(pad[i][:, 0:32], 0.0),)
            ms = [scr.take() for _ in range(4)]
            mt = [S.dma(ms[i].ap.rearrange("p (k t) -> p k t", k=2), a["mem"][:, 2 * i:2 * i + 2, :], ms[i].sem,
                        w=tuple(ms[i].free)) for i in range(4)]
            chunks = [ms[k // 2].ap[:, 256 * (k % 2):256 * (k % 2) + 256] for k in range(8)]
            nh = [region(256 * k, 256) for k in range(8)]
            nl = [region(2048 + 256 * k, 256) for k in range(8)]
            hm = norm(chunks, [mt[k // 2] for k in range(8)], [prm("g_mem_2", k) for k in range(8)], nh, nl, 256,
                      free=(p0,))
            for s in ms:
                s.give(hm[7])
            hx = norm(X, xt, [prm("g_mix_2", k) for k in range(8)], Hh, Hl, T, free=(p0,))
            yh = [region(512 * c, 512) for c in range(8)]
            yl = [region(4096 + 512 * c, 512) for c in range(8)]
            kh, kl, vh, vl = (region(8192 + 512 * i, 512) for i in range(4))
            qs = Slots([Slot((region(10240 + 1024 * i, 512), region(10752 + 1024 * i, 512))) for i in range(2)])
            mkh, mkl = ([region(12288 + 512 * j + 256 * c, 256) for c in range(2)] for j in range(2))
            mvh, mvl = ([region(13312 + 512 * j + 256 * c, 256) for c in range(2)] for j in range(2))
            for i, s in enumerate(dts.slots):
                s.free = (p0,)
            for s in qs.slots:
                s.free = (p0,)
            y_tok = [None] * 8

            def pnorm(b, t, gain, n, hi, lo, rope, free):
                n7 = bank[7]
                n7.held = True
                t1 = sums([b.ap[:, 0:n]], [t], blk, n7, n)
                r, t1 = rstd(n7, n, 64, t1)
                t2 = V.stt(r.ap[:, 0:n], b.ap[:, 0:n], gain, r.ap[:, 0:n], ALU.mult, ALU.mult, w=(t1,))
                b.give(t2)
                if rope:
                    n7.held = True
                    t3 = P.mm(n7.ap, perm, r.ap, True, True, w=(t2,) + tuple(n7.free), inc=True)
                    s = scr.take()
                    t4 = V.tt(s.ap, n7.ap, cos_t[:, 512:1024], ALU.mult, w=(t3, rope_tok) + tuple(s.free))
                    n7.give(t4)
                    t2 = V.tt(r.ap, r.ap, cos_t[:, 0:512], ALU.mult, w=(t3,))
                    t2 = V.tt(r.ap, r.ap, s.ap, ALU.add, w=(t2, t4))
                    s.give(t2)
                t3 = parts(r.ap[:, 0:n], hi, lo, w=(t2,), free=free)
                r.give(t3)
                return t3

            mk_tok, mv_tok = [], []
            for c in range(4):
                b = bank[c % 2]
                t = linear("w_mkv", c, b, nh, nl, hm, n=256)
                if c < 2:
                    mk_tok.append(pnorm(b, t, prm("g_mk_2"), 256, mkh[c], mkl[c], False, (p0,)))
                else:
                    mv_tok.append(to_rows(b, t, mvh[c - 2], mvl[c - 2], (p0,), n=2))
            mem_done = u_last(P)
            b = bank[0]
            t = linear("w_in2", 4, b, Hh, Hl, hx)
            k_tok = pnorm(b, t, prm("g_k_2"), T, kh, kl, True, (p0,))
            b = bank[1]
            t = linear("w_in2", 5, b, Hh, Hl, hx)
            v_tok = to_rows(b, t, vh, vl, (p0,))

            cy = []
            for c in range(2):
                b = bank[0]
                t = linear("w_in2", 6 + c, b, Hh, Hl, hx)
                b2 = bank[1]
                t2 = linear("w_in2", 8 + c, b2, Hh, Hl, hx)
                s = scr.take()
                ts_ = A.act(s.ap, b2.ap, ACT.Sigmoid, w=(t2,) + tuple(s.free))
                b2.give(ts_)
                tp = V.tt(pad[c][:, 32:544], s.ap, b.ap, ALU.mult, w=(t, ts_) + tuple(pad_free[c]))
                b.give(tp)
                s.give(tp)
                cy.append((scr.take(), tp))

            def conv():
                toks = []
                for c in range(2):
                    y, t = cy[c]
                    wd = [prm("w_dw_2", 31 * c + j) for j in range(31)]
                    t = V.ts(y.ap, pad[c][:, 32:544], wd[30], prm("b_dw_2", c), ALU.mult, ALU.add,
                             w=(t,) + tuple(y.free))
                    for j in range(30):
                        t = V.stt(y.ap, pad[c][:, 2 + j:514 + j], wd[j], y.ap, ALU.mult, ALU.add, w=(t,))
                        if j % 3 == 2:
                            yield
                    toks.append(t)
                n7 = bank[7]
                n7.held = True
                for c in range(2):
                    p = P.mm(n7.ap, ones, cy[c][0].ap, c == 0, c == 1, w=(toks[c],) + tuple(n7.free), inc=True)
                for c in range(2):
                    t = V.stt(cy[c][0].ap, n7.ap, -1.0 / 256, cy[c][0].ap, ALU.mult, ALU.add, w=(p,))
                    toks[c] = t
                n7.give(t)
                n7.held = True
                t = sums([cy[c][0].ap for c in range(2)], toks, ones, n7, T)
                r, t = rstd(n7, T, 256, t)
                for c in range(2):
                    y = cy[c][0]
                    t1 = V.stt(y.ap, y.ap, prm("g_conv_ln_2", c), r.ap, ALU.mult, ALU.mult, w=(t,))
                    t1 = A.act(y.ap, y.ap, ACT.Silu, w=(t1,), bias=prm("b_conv_ln_2", c))
                    t2 = parts(y.ap, yh[4 + c], yl[4 + c], w=(t1,), free=(mem_done,))
                    y.give(t2)
                    y_tok[4 + c] = t2
                r.give(t1, t2)

            sb2 = Slots([Slot([bank[2], bank[3]]), Slot([bank[4], bank[5]])])
            for s in sb2.slots:
                s.free = tuple(t for b in s.ap for t in b.free)

            def heads(c, sink, row, qd, q_tok, keys, key_tok, vals_, val_tok, local):
                ob = bank[1]
                sx = scr.take()
                for qb in range(4):
                    lo_k = 0 if not local or qb == 0 else 128 * (qb - 1)
                    n = 256 if not local or qb else 128
                    sb = sb2.take()
                    qs_ = slice(128 * qb, 128 * qb + 128)
                    for e in range(2):
                        r = slice(64 * e, 64 * e + 64)
                        b = sb.ap[e].ap
                        t = P.mm3(b[:, 0:n], qd.ap[0][r, qs_], qd.ap[1][r, qs_], keys[0][r, lo_k:lo_k + n],
                                  keys[1][r, lo_k:lo_k + n], True, not local, w=(q_tok, key_tok) + tuple(sb.free),
                                  inc=not local)
                        if local:
                            t = P.mm(b[:, 0:n], idb_t[:, :], m2b_t[:, 256 - n:256], False, True,
                                     w=(masks,), inc=True)
                    last_q = t
                    small = 96 if qb % 2 else 112
                    ps, rc, t = soft(sb, t, n, 0.125, small, sink)
                    for e in range(2):
                        t = V.ts(ps[e].ap[:, 0:n], ps[e].ap[:, 0:n], rc[:, e:e + 1], None, ALU.mult, w=(t,))
                    sm_free[small] = (t,)
                    yield
                    ds_ = []
                    nb = n // 128
                    b6 = bank[6]
                    b6.held = True
                    for e in range(2):
                        for k in range(nb):
                            col = 256 * e + 128 * k
                            tp = P.tr(b6.ap[:, col:col + 128], ps[e].ap[:, 128 * k:128 * k + 128], ident,
                                      w=(t,) + (tuple(b6.free) if e == 0 and k == 0 else ()),
                                      inc=True)
                    ps[0].give(tp)
                    ps[1].give(tp)
                    d = dts.take()

                    def v2(z):
                        return z.rearrange("p (e k) -> p e k", e=2)[:, :, 0:n]
                    t = parts(v2(b6.ap), v2(d.ap[0]), v2(d.ap[1]), w=(tp,), free=tuple(d.free))
                    b6.give(t)
                    yield
                    o0 = bank[0]
                    while ob.held or o0.held:
                        yield
                    ob.held = o0.held = True
                    for e, bo in ((0, o0), (1, ob)):
                        for k in range(nb):
                            vi = lo_k // 128 + k
                            cs = slice(256 * e + 128 * k, 256 * e + 128 * k + 128)
                            t2 = P.mm3(bo.ap[:, 0:128], vals_[0][vi], vals_[1][vi], d.ap[0][:, cs], d.ap[1][:, cs],
                                       k == 0, k == nb - 1, w=(t, val_tok) + tuple(bo.free), inc=k == nb - 1)
                    d.give(t2)
                    A.wait(tuple(sx.free))
                    t3 = A.copy(sx.ap[0:64, qs_], o0.ap[0:64, 0:128], w=(t2,))
                    t3 = A.copy(sx.ap[64:128, qs_], ob.ap[64:128, 0:128])
                    o0.give(t3)
                    ob.give(t3)
                qd.give(last_q)
                t = parts(sx.ap, yh[row], yl[row], w=(t3,), free=(mem_done,))
                sx.give(t)
                y_tok[row] = t

            cv = conv()
            vt = ([vh[:, 128 * k:128 * k + 128] for k in range(4)], [vl[:, 128 * k:128 * k + 128] for k in range(4)])

            def q_proj(i):
                b = bank[0]
                name = (0, 1, 2, 3, 10, 11)[i]
                t = linear("w_in2", name, b, Hh, Hl, hx)
                qd = qs.take()
                gain = prm("g_q_2") if i < 4 else prm("g_mq_2")
                t = pnorm(b, t, gain, T, qd.ap[0], qd.ap[1], i < 4, tuple(qd.free))
                return qd, t

            nxt = q_proj(0)
            for i in range(6):
                qd, qt = nxt
                if i < 4:
                    gen = heads(i, prm("sinks_2", 2 * i, 2), i, qd, qt, (kh, kl), k_tok, vt, v_tok, True)
                else:
                    c = i - 4
                    mv = tuple([z[c][:, 128 * k:128 * k + 128] for k in range(2)] for z in (mvh, mvl))
                    gen = heads(c, None, 6 + c, qd, qt, (mkh[c], mkl[c]), mk_tok[c], mv, mv_tok[c], False)
                if i < 5:
                    nxt = q_proj(i + 1)
                for _ in gen:
                    next(cv, None)
            for _ in cv:
                pass
            xl = []
            for m in range(8):
                b = bank[m % 2]
                t = linear("w_out2", m, b, yh, yl, y_tok)
                t2 = V.tt(X[m], X[m], b.ap, ALU.add, w=(t, hx[7]))
                b.give(t2)
                xl.append(t2)
            for s, (b0, b1) in zip(sb2.slots, ((2, 3), (4, 5))):
                for i in (b0, b1):
                    bank[i].free = tuple(bank[i].free) + tuple(s.free)
            return xl

        def tail():
            if stop_after == "first":
                return x1
            x2 = peer()
            if stop_after == "peer":
                return x2
            x3 = ffn("1", "g_ffn1_2", x2)
            if stop_after == "ffn1":
                return x3
            x4 = mixer(x3)
            if stop_after == "mix":
                return x4
            return ffn("2", "g_ffn2_2", x4)

        for s in sbank.slots:
            for b in s.ap:
                b.free = tuple(b.free) + tuple(s.free)
        finish(tail())

        block = ctx.enter_context(nc.Block())

        @block.sync
        def _(eng):
            S.emit(eng)

        @block.scalar
        def _(eng):
            A.emit(eng)

        @block.vector
        def _(eng):
            V.emit(eng)

        @block.gpsimd
        def _(eng):
            G.emit(eng)

        @block.tensor
        def _(eng):
            P.emit(eng)


def _layout(inputs):
    import numpy as np
    z = {k: np.asarray(v) for k, v in inputs.items()}
    f32 = np.float32

    def tiles(w):
        k, n = w.shape
        return np.ascontiguousarray(
            w.reshape(k // 128, 128, n // 128, 128).transpose(2, 1, 0, 3).reshape(n // 128, 128, k))

    def cols(v):
        v = v.reshape(-1)
        if v.size < 128:
            v = np.tile(v, 128 // v.size)
        return v.reshape(-1, 128).T

    d = {}
    d["x"] = np.ascontiguousarray(z["x"][0].T.reshape(8, 128, T).transpose(1, 0, 2))
    d["mem"] = np.ascontiguousarray(z["mem_2"][0].T.reshape(8, 128, 256).transpose(1, 0, 2))
    d["pos"] = np.ascontiguousarray(np.broadcast_to(z["positions_2"][0], (128, T)))
    d["lambdas"] = np.ascontiguousarray(np.broadcast_to(np.concatenate(
        [z[n][0] for n in ("lambda_q1", "lambda_k1", "lambda_q2", "lambda_k2")]), (128, 256)))
    d["w_in"] = tiles(z["w_in"][0])
    wa, wx = z["w_rg_a"][0], z["w_rg_x"][0]
    rg = np.zeros((10, 128, 256), f32)
    for c in range(10):
        for j, w in enumerate((wa, wx)):
            rg[c, 0:64, 128 * j:128 * j + 64] = w[2 * c]
            rg[c, 64:128, 128 * j + 64:128 * j + 128] = w[2 * c + 1]
    d["w_rg"] = rg
    d["w_brr"] = np.ascontiguousarray(
        tiles(z["w_br_rnn"][0]).reshape(8, 128, 2, 640).transpose(0, 2, 1, 3).reshape(16, 128, 640))
    d["w_bra"] = tiles(z["w_br_attn"][0])
    d["w_out"] = tiles(z["w_out"][0])
    d["w_pq"] = tiles(z["w_peer_q"][0])
    d["sk"] = np.ascontiguousarray(z["peer_sub_keys"][0].reshape(16, 128, 128).transpose(0, 2, 1))
    d["pu"] = np.ascontiguousarray(
        z["peer_u"][0].reshape(128, 128, 8, 128).transpose(0, 3, 2, 1).reshape(128, 128, 1024))
    d["pv"] = np.ascontiguousarray(
        z["peer_v"][0].reshape(16, 4, 2, 128, 2, 512).transpose(0, 4, 1, 3, 2, 5).reshape(128, 128, 1024))
    for fo, nm in (("1", "ffn1"), ("2", "ffn2")):
        d["wg" + fo] = tiles(z[f"w_{nm}_gate_2"][0])
        d["wu" + fo] = tiles(z[f"w_{nm}_up_2"][0])
        wd = tiles(z[f"w_{nm}_down_2"][0])
        full = np.zeros((24, 128, 1024), f32)
        for gi, (first, n) in enumerate(FG):
            full[8 * gi:8 * gi + 8, :, 0:128 * n] = wd[:, :, 128 * first:128 * (first + n)]
        d["wd" + fo] = full
    w2 = z["w_in_2"][0]
    order = [h for c in range(4) for h in (c, c + 4)]
    q2 = w2[:, 0:512].reshape(D, 8, 64)[:, order].reshape(D, 512)
    d["w_in2"] = tiles(np.concatenate([q2, w2[:, 512:]], axis=1))
    wo = z["w_out_2"][0]
    d["w_out2"] = tiles(np.concatenate([wo[0:512].reshape(8, 64, D)[order].reshape(512, D), wo[512:]], axis=0))
    d["w_mkv"] = tiles(z["w_mem_kv_2"][0])
    p = np.zeros((128, NP), f32)

    def setc(name, v):
        p[:, PCOLS[name]:PCOLS[name] + v.shape[1]] = v

    for n in ("norm1_g", "b_gate", "q_norm_g", "k_norm_g", "subln_g", "conv_b", "b_rg_a", "b_rg_x", "rg_lambda",
              "norm2_g", "g_ffn1_2", "g_mix_2", "g_q_2", "g_k_2", "b_dw_2", "g_conv_ln_2", "b_conv_ln_2",
              "g_mem_2", "g_mq_2", "g_mk_2", "g_ffn2_2"):
        setc(n, cols(z[n][0]))
    setc("conv_w", z["conv_w"][0].T.reshape(10, 128, 4).transpose(1, 0, 2).reshape(128, 40))
    setc("w_dw_2", z["w_dw_2"][0].T.reshape(2, 128, 31).transpose(1, 0, 2).reshape(128, 62))
    setc("sinks_2", np.broadcast_to(z["sinks_2"][0][order], (128, 8)))
    d["prm"] = p
    c = np.zeros((128, NC_), f32)
    i = np.arange(128)
    c[:, C_ID:C_ID + 128] = np.eye(128)
    c[:, C_ONE:C_ONE + 128] = 1
    c[:, C_BLK:C_BLK + 128] = (i[:, None] // 64) == (i[None, :] // 64)
    c[:, C_IOTA:C_IOTA + 128] = i[None, :]
    for b in (0, 64):
        for j in range(8):
            c[b + j + 8, C_PERM + b + j] = -1
            c[b + j, C_PERM + b + j + 8] = 1
            c[b + j, C_INVF] = c[b + j + 8, C_INVF] = INV_FREQ[j]
    c[:, C_MASK2:C_MASK2 + 128] = np.where(i[None, :] > i[:, None], 0, -1e30)
    c[:, C_MASK2 + 128:C_MASK2 + 256] = np.where(i[None, :] <= i[:, None], 0, -1e30)
    c[0:64, C_MASK1:C_MASK1 + 64] = -1e30
    c[:, C_EPS] = EPS
    c[:, C_EPS2] = EPS / 0.64
    c[:, C_HPI] = np.pi / 2
    d["cst"] = c
    return d


def kernel(**inputs):
    import numpy as _np
    import concourse.bacc as _bacc
    from concourse import mybir as _mybir
    from concourse.bass_utils import run_bass_kernel_spmd as _run

    nc = _bacc.Bacc("TRN2", target_bir_lowering=False, num_devices=1)
    arrays, args = {}, {}
    for name, v in _layout(inputs).items():
        v = _np.ascontiguousarray(v)
        arrays[f"in_{name}"] = v
        args[name] = nc.dram_tensor(f"in_{name}", v.shape, _mybir.dt.from_np(v.dtype), kind="ExternalInput").ap()
    out = nc.dram_tensor("out_x", (D, T), F32, kind="ExternalOutput").ap()
    build(nc, args, out)
    r = _run(nc, [arrays], core_ids=[0])
    return _np.ascontiguousarray(r.results[0]["out_x"].T).reshape(1, T, D)
```

```python
from contextlib import ExitStack

import concourse.bass as bass
from concourse import mybir

F32 = mybir.dt.float32
F32R = mybir.dt.float32r
BF16 = mybir.dt.bfloat16
U32 = mybir.dt.uint32
I32 = mybir.dt.int32
ALU = mybir.AluOpType
ACT = mybir.ActivationFunctionType
AX_X = mybir.AxisListType.X

T = 512
D = 1024
EPS = 1e-6
LAM_INIT = 0.2
INV_FREQ = [1.0, 0.1939227432012558, 0.03760603070259094, 0.007292664609849453,
            0.0014142135623842478, 0.00027424818836152554, 5.3182957344688475e-05,
            1.0313385246263351e-05]

PCOLS = {}


def _cols():
    at = 0
    for name, n in (("norm1_g", 8), ("b_gate", 16), ("q_norm_g", 1), ("k_norm_g", 1), ("subln_g", 1),
                    ("conv_w", 40), ("conv_b", 10), ("b_rg_a", 10), ("b_rg_x", 10), ("rg_lambda", 10),
                    ("norm2_g", 8), ("g_ffn1_2", 8), ("g_mix_2", 8), ("g_q_2", 1), ("g_k_2", 1),
                    ("sinks_2", 8), ("w_dw_2", 62), ("b_dw_2", 2), ("g_conv_ln_2", 2),
                    ("b_conv_ln_2", 2), ("g_mem_2", 8), ("g_mq_2", 1), ("g_mk_2", 1), ("g_ffn2_2", 8)):
        PCOLS[name] = at
        at += n
    return at


NP = _cols()
C_ID, C_ONE, C_BLK, C_IOTA, C_PERM, C_MASK2, C_MASK1, C_INVF, C_EPS, C_EPS2, C_HPI, NC_ = (
    0, 128, 256, 384, 512, 640, 896, 960, 961, 962, 963, 964)

FG = [(0, 8), (8, 8), (16, 6)]


def unit_order():
    u = []
    for c in range(0, 12, 2):
        if c < 10:
            u += [("w_in", x + c + i, 1024) for i in range(2) for x in (24, 34)]
        if c:
            u += [("w_rg", c - 2 + i, 256) for i in range(2)]
    for m in range(8):
        u += [("w_in", 52 + m, 1024), ("w_brr", 2 * m, 640), ("w_brr", 2 * m + 1, 640)]
    for h in range(8):
        u += [("w_in", h, 1024), ("w_in", 8 + h, 1024), ("w_in", 16 + h, 1024)]
    for m in range(8):
        u += [("w_in", 44 + m, 1024), ("w_bra", m, 1024)]
    u += [("w_out", m, 1024) for m in range(8)]
    U = [("pu", i, 1024) for i in range(128)]
    for j in range(16):
        u += [("w_pq", j, 1024), U.pop(0), U.pop(0), ("sk", j, 128), U.pop(0)]
        if j % 2:
            u += [U.pop(0) for _ in range(4)]
    u += U
    for g in range(16):
        for half in range(2):
            u += [("pv", (g * 2 + half) * 4 + p, 1024) for p in range(4)]
    for f in ("1", "2"):
        if f == "2":
            u += [("w_in2", c, 1024) for c in (4, 5, 6, 8, 7, 9, 0)]
            u += [("w_mkv", c, 1024) for c in range(4)]
            u += [("w_in2", c, 1024) for c in (1, 2, 3, 10, 11)]
            u += [("w_out2", m, 1024) for m in range(8)]
        for gi in range(4):
            if gi < 3:
                for i in range(FG[gi][0], sum(FG[gi])):
                    u += [("wg" + f, i, 1024), ("wu" + f, i, 1024)]
            if gi > 0:
                u += [("wd" + f, (gi - 1) * 8 + m, FG[gi - 1][1] * 128) for m in range(8)]
    return u


class Queue:

    def __init__(self, sem):
        self.sem, self.items, self.n, self.seen = sem, [], 0, {}

    def wait(self, toks):
        for t in toks:
            if t is None:
                continue
            sem, v = t
            if self.seen.get(id(sem), 0) < v:
                self.seen[id(sem)] = v
                self.items.append((0, sem, v))

    def put(self, f, w=(), inc=True):
        self.wait(w)
        self.items.append((1, f, inc))
        if inc:
            self.n += 1
            return (self.sem, self.n)
        return None

    def emit(self, eng):
        for kind, a, b in self.items:
            if kind == 0:
                eng.wait_ge(a, b)
            elif kind == 2:
                a(eng).then_inc(b, 16)
            elif b:
                a(eng).then_inc(self.sem, 1)
            else:
                a(eng)


class Vec(Queue):
    def tt(self, out, a, b, op, w=()):
        return self.put(lambda e: e.tensor_tensor(out, a, b, op), w)

    def ts(self, out, a, s1, s2, op0, op1=None, w=()):
        if op1 is None:
            return self.put(lambda e: e.tensor_scalar(out, a, s1, None, op0), w)
        return self.put(lambda e: e.tensor_scalar(out, a, s1, s2, op0, op1), w)

    def stt(self, out, a, s, b, op0, op1, w=()):
        return self.put(lambda e: e.scalar_tensor_tensor(out=out, in0=a, scalar=s, in1=b, op0=op0, op1=op1), w)

    def recip(self, out, a, w=()):
        return self.put(lambda e: e.reciprocal(out, a), w)

    def copy(self, out, a, w=()):
        return self.put(lambda e: e.tensor_copy(out, a), w)

    def red(self, out, a, op, w=()):
        return self.put(lambda e: e.tensor_reduce(out, a, AX_X, op), w)

    def max8(self, out, a, w=()):
        return self.put(lambda e: e.max(out, a), w)

    def idx8(self, out, m, a, w=()):
        return self.put(lambda e: e.max_index(out, m, a), w)

    def rep8(self, out, m, a, w=()):
        return self.put(lambda e: e.match_replace(out, m, a, -3.0e38), w)

    def scan(self, out, a, b, w=()):
        return self.put(lambda e: e.tensor_tensor_scan(out, a, b, 0.0, ALU.mult, ALU.add), w)

    def fill(self, out, v, w=()):
        return self.put(lambda e: e.memset(out, v), w)


class Act(Queue):
    def act(self, out, a, func, w=(), scale=1.0, bias=None, acc=None):
        if bias is None:
            if acc is None:
                return self.put(lambda e: e.activation(out, a, func, scale=scale), w)
            return self.put(lambda e: e.activation(out, a, func, scale=scale, accum_out=acc), w)
        if acc is None:
            return self.put(lambda e: e.activation(out, a, func, bias=bias, scale=scale), w)
        return self.put(lambda e: e.activation(out, a, func, bias=bias, scale=scale, accum_out=acc), w)

    def copy(self, out, a, w=()):
        return self.put(lambda e: e.activation(out, a, ACT.Copy), w)


class Ten(Queue):
    def mm(self, out, l, r, start, stop, w=(), inc=False):
        return self.put(lambda e: e.matmul(out, l, r, start=start, stop=stop, skip_group_check=True), w, inc)

    def mm3(self, out, lh, ll, rh, rl, start, stop, w=(), inc=False):
        self.mm(out, lh, rh, start, False, w)
        self.mm(out, lh, rl, False, False)
        return self.mm(out, ll, rh, False, stop, (), inc)

    def tr(self, out, a, ident, w=(), inc=False):
        return self.put(lambda e: e.transpose(out, a, ident), w, inc)


class Sync(Queue):
    def dma(self, out, a, sem, w=()):
        self.wait(w)
        self.items.append((2, lambda e: e.dma_start(out, a), sem[0]))
        sem[1] += 16
        return (sem[0], sem[1])


class Slot:
    def __init__(self, ap, sem=None):
        self.ap, self.free, self.held, self.sem = ap, (), False, sem

    def give(self, *toks):
        assert self.held
        self.held, self.free = False, toks


class Slots:

    def __init__(self, slots):
        self.slots, self.i = slots, 0

    def take(self):
        for _ in range(len(self.slots)):
            s = self.slots[self.i % len(self.slots)]
            self.i += 1
            if not s.held:
                s.held = True
                return s
        raise AssertionError("no free slot")


def f(ap):
    return ap.bitcast(F32)


def build(nc, a, out, stop_after=None, dbg=None):
    with ExitStack() as ctx:
        nsem = [0]

        def sem():
            nsem[0] += 1
            return ctx.enter_context(nc.semaphore(f"s{nsem[0]}"))

        base = 16512
        pos = [base]

        def at(name, cols, dt, offset=None, size=4):
            off = pos[0] if offset is None else offset
            t = nc.alloc_sbuf_tensor_at(name, [128, cols], dt, offset=off)
            if offset is None:
                pos[0] += (cols * size + 31) // 32 * 32
            return t, off

        NRAW, NW = 5, 5
        raw_t, _ = at("raw", NRAW * 1024, F32)
        whl_t, _ = at("whl", NW * 2048, F32R)
        X_t, _ = at("X", 4096, F32)
        H_t, h_off = at("H", 8192, F32R)
        GA_t, _ = at("GA", 8192, F32, offset=h_off)
        S_t, s_off = at("S", 16384, F32R)
        ST_t, _ = at("ST", 16384, F32, offset=s_off)
        scr_t, _ = at("scr", 10 * 512, F32)
        pad_t, _ = at("pad", 2 * 544, F32)
        scr_off = pos[0] - 10 * 2048 - 2 * 544 * 4
        pad_off = pos[0] - 2 * 544 * 4
        cst_t, _ = at("cst", NC_, F32)
        prm_t, _ = at("prm", NP, F32)
        cos_t, cos_off = at("rope", 1024, F32)
        oh_t = [at(n, c, F32R, offset=o)[0]
                for n, c, o in (("oh_scr", 10 * 512, scr_off), ("oh_pad", 2 * 544, pad_off), ("oh_rope", 1024, cos_off))]
        idb_t, _ = at("idb", 128, BF16, size=2)
        m2b_t, _ = at("m2b", 256, BF16, size=2)
        m1b_t, _ = at("m1b", 64, BF16, size=2)
        sm_t, _ = at("sm", 256, F32)
        su_t, _ = at("su", 256, U32)
        assert pos[0] <= nc.sbuf_usable_end
        pb = [ctx.enter_context(nc.psum_tensor(f"pb{i}", [128, 512], F32)) for i in range(8)]
        gd = nc.dram_tensor("gd", [128, 128, 512], F32).ap()
        ad = nc.dram_tensor("ad", [128, 128, 512], F32).ap()

        V, A, P, G, S = Vec(sem()), Act(sem()), Ten(sem()), Vec(sem()), Sync(sem())

        def cst(c, n):
            return cst_t[:, c:c + n]

        def prm(name, i=0, n=1):
            return prm_t[:, PCOLS[name] + i:PCOLS[name] + i + n]

        ident, ones, blk, iota = cst(C_ID, 128), cst(C_ONE, 128), cst(C_BLK, 128), cst(C_IOTA, 128)
        perm, invf, eps, eps2, hpi = cst(C_PERM, 128), cst(C_INVF, 1), cst(C_EPS, 1), cst(C_EPS2, 1), cst(C_HPI, 1)
        X = [X_t[:, 512 * k:512 * k + 512] for k in range(8)]
        Hh = [H_t[:, 512 * k:512 * k + 512] for k in range(8)]
        Hl = [H_t[:, 4096 + 512 * k:4096 + 512 * k + 512] for k in range(8)]
        scr = Slots([Slot(scr_t[:, 512 * i:512 * i + 512], [sem(), 0]) for i in range(10)])
        bank = [Slot(pb[i][:, :]) for i in range(8)]

        units = unit_order()
        wsem = [[sem(), 0] for _ in range(NRAW)]
        raw_free = [() for _ in range(NRAW)]
        part_free = [() for _ in range(NW)]
        st = {"dma": 0, "split": 0, "get": 0}
        landed, parted = {}, {}

        def w_load():
            j = st["dma"]
            if j >= len(units):
                return
            name, i, n = units[j]
            r = j % NRAW
            landed[j] = S.dma(raw_t[:, r * 1024:r * 1024 + n], a[name][i, :, 0:n], wsem[r], w=raw_free[r])
            st["dma"] += 1

        def w_split():
            j = st["split"]
            if j >= len(units):
                return
            n = units[j][2]
            r, q = j % NRAW, j % NW
            src = raw_t[:, r * 1024:r * 1024 + n]
            hi = whl_t[:, q * 2048:q * 2048 + n]
            lo = whl_t[:, q * 2048 + 1024:q * 2048 + 1024 + n]
            assert part_free[q] is not None
            t1 = A.copy(hi, src, w=(landed[j],) + part_free[q])
            t2 = V.tt(lo, src, f(hi), ALU.subtract, w=(t1,))
            parted[j] = (hi, lo, t2)
            part_free[q] = None
            raw_free[r] = (t2,)
            st["split"] += 1
            w_load()

        def w_get(name, i):
            j = st["get"]
            assert units[j][:2] == (name, i), (units[j], name, i)
            while st["split"] < min(j + NW, len(units)):
                w_split()
            st["get"] += 1
            hi, lo, t = parted.pop(j)
            return hi, lo, t, j

        def w_done(j, tok):
            part_free[j % NW] = (tok,)

        c_sem, p_sem, x_sem = [sem(), 0], [sem(), 0], [[sem(), 0] for _ in range(4)]

        def load_x(w=()):
            return [S.dma(X_t[:, 1024 * i:1024 * i + 1024].rearrange("p (k t) -> p k t", k=2),
                          a["x"][:, 2 * i:2 * i + 2, :], x_sem[i], w=w) for i in range(4)]

        c_in = S.dma(cst_t[:, :], a["cst"], c_sem)
        x_in = load_x()
        p_in = S.dma(prm_t[:, :], a["prm"], p_sem)
        for _ in range(NRAW):
            w_load()
        lam_s = scr.take()
        lam_in = S.dma(lam_s.ap[:, 0:256], a["lambdas"], lam_s.sem)
        V.copy(idb_t[:, :], ident, w=(c_in, p_in))
        V.copy(m2b_t[:, :], cst(C_MASK2, 256))
        masks = V.copy(m1b_t[:, :], cst(C_MASK1, 64))
        for e in (A, P, G):
            e.wait((c_in,))

        def sums(chunks, toks, lhs, b, n):
            last = None
            for k, c in enumerate(chunks):
                s = scr.take()
                t = A.act(s.ap[:, 0:n], c, ACT.Square, w=(toks[k],) + tuple(s.free))
                last = P.mm(b.ap[:, 0:n], lhs, s.ap[:, 0:n], k == 0, k == len(chunks) - 1,
                            w=(t,) + (tuple(b.free) if k == 0 else ()), inc=True)
                s.give(last)
            return last

        def rstd(b, n, width, tok, gain=1.0, bias=None):
            r = scr.take()
            t = A.act(r.ap[:, 0:n], b.ap[:, 0:n], ACT.Sqrt, w=(tok,) + tuple(r.free),
                      scale=gain / width, bias=eps if bias is None else bias)
            b.give(t)
            t = V.recip(r.ap[:, 0:n], r.ap[:, 0:n], w=(t,))
            return r, t

        def norm(chunks, toks, gains, hi, lo, n, free=()):
            b = bank[7]
            assert not b.held
            b.held = True
            t = sums(chunks, toks, ones, b, n)
            r, t = rstd(b, n, D, t)
            res, prev = [], None
            for k in range(len(chunks) + 1):
                if k < len(chunks):
                    s = scr.take()
                    t1 = V.stt(s.ap[:, 0:n], chunks[k], gains[k], r.ap[:, 0:n], ALU.mult, ALU.mult,
                               w=(t,) + tuple(s.free))
                    t2 = A.copy(hi[k], s.ap[:, 0:n], w=(t1,) + tuple(free))
                if prev is not None:
                    s0, k0, h0 = prev
                    t3 = V.tt(lo[k0], s0.ap[:, 0:n], f(hi[k0]), ALU.subtract, w=(h0,) + tuple(free))
                    s0.give(t3)
                    res.append(t3)
                prev = (s, k, t2) if k < len(chunks) else None
            r.give(res[-1])
            return res

        def linear(name, i, b, hh, hl, toks, n=T, w=(), start=True, stop=True, kk=8, take=True):
            hi, lo, t, j = w_get(name, i)
            if take:
                assert not b.held
                b.held = True
                w = tuple(w) + tuple(b.free)
            for k in range(kk):
                last = P.mm3(b.ap[:, 0:n], hi[:, 128 * k:128 * k + 128], lo[:, 128 * k:128 * k + 128],
                             hh[k], hl[k], start and k == 0, stop and k == kk - 1,
                             w=((t,) + tuple(w) if k == 0 else ()) + (toks[k],), inc=k == kk - 1)
            w_done(j, last)
            return last

        def linear_g(name, i, b, hh, hl, toks, n=T, cuts=(4,)):
            hi, lo, t, j = w_get(name, i)
            for k in range(8):
                if k in cuts:
                    yield
                last = P.mm3(b.ap[:, 0:n], hi[:, 128 * k:128 * k + 128], lo[:, 128 * k:128 * k + 128],
                             hh[k], hl[k], k == 0, k == 7,
                             w=((t,) + tuple(b.free) if k == 0 else ()) + (toks[k],), inc=k == 7)
            w_done(j, last)
            return last

        def yield_all(g):
            while True:
                try:
                    next(g)
                except StopIteration as e:
                    return e.value

        def parts(src, hi, lo, w=(), free=()):
            t = A.copy(hi, src, w=tuple(w) + tuple(free))
            return V.tt(lo, src, f(hi), ALU.subtract, w=(t,) + tuple(w))

        lm = lam_s.ap
        t = V.tt(sm_t[:, 128:192], lm[:, 0:64], lm[:, 64:128], ALU.mult, w=(lam_in,))
        t = V.tt(sm_t[:, 192:256], lm[:, 128:192], lm[:, 192:256], ALU.mult)
        lam_s.give(t)
        t = V.red(sm_t[:, 0:1], sm_t[:, 128:192], ALU.add, w=(t,))
        t = V.red(sm_t[:, 1:2], sm_t[:, 192:256], ALU.add)
        t = A.act(sm_t[:, 2:4], sm_t[:, 0:2], ACT.Exp, w=(t,))
        t = V.tt(sm_t[:, 4:5], sm_t[:, 2:3], sm_t[:, 3:4], ALU.subtract, w=(t,))
        neglam = sm_t[:, 5:6]
        t = V.ts(neglam, sm_t[:, 4:5], LAM_INIT, -1.0, ALU.add, ALU.mult, w=(t,))
        lam = prm("rg_lambda", 0, 10)
        q = [sm_t[:, 16 + 10 * i:26 + 10 * i] for i in range(6)]
        nsp, nsp2 = q[4], q[5]
        t = V.ts(q[0], lam, -1.0, None, ALU.mult, w=(p_in,))
        t = V.tt(q[1], lam, q[0], ALU.min, w=(t,))
        t = A.act(q[1], q[1], ACT.Exp, w=(t,))
        t = V.ts(q[2], q[1], 2.0, None, ALU.add, w=(t,))
        t = V.recip(q[2], q[2], w=(t,))
        t = V.tt(q[1], q[1], q[2], ALU.mult, w=(t,))
        t = V.tt(q[2], q[1], q[1], ALU.mult, w=(t,))
        t = V.ts(q[3], q[2], 1.0 / 19, 1.0 / 17, ALU.mult, ALU.add, w=(t,))
        for d in (15, 13, 11, 9, 7, 5, 3, 1):
            t = V.tt(q[3], q[3], q[2], ALU.mult, w=(t,))
            t = V.ts(q[3], q[3], 1.0 / d, None, ALU.add, w=(t,))
        t = V.stt(q[3], q[3], 2.0, q[1], ALU.mult, ALU.mult, w=(t,))
        t = V.stt(q[3], q[0], 0.0, q[3], ALU.max, ALU.add, w=(t,))
        sp_tok = V.ts(nsp, q[3], -8.0, None, ALU.mult, w=(t,))
        A.wait((sp_tok,))

        x_tok = [x_in[k // 2] for k in range(8)]
        pad = [pad_t[:, 544 * i:544 * i + 544] for i in range(2)]
        pad0 = [V.fill(pad[i][:, 0:32], 0.0) for i in range(2)]
        pad_free = [(), ()]

        h1 = norm(X, x_tok, [prm("norm1_g", k) for k in range(8)], Hh, Hl, T)

        def rope_tables():
            pos_s = scr.take()
            pos_in = S.dma(pos_s.ap.bitcast(I32), a["pos"], pos_s.sem, w=tuple(pos_s.free))
            s = [scr.take() for _ in range(3)]
            ang, n, r = s[0].ap, s[1].ap, s[2].ap
            t = V.copy(n, pos_s.ap.bitcast(I32), w=(pos_in,) + tuple(s[1].free))
            pos_s.give(t)
            t = V.ts(ang, n, invf, None, ALU.mult, w=(t,) + tuple(s[0].free))
            t = V.ts(n, ang, 0.15915494309189535, None, ALU.mult, w=(t,))
            t = V.ts(n, n, 12582912.0, None, ALU.add, w=(t,))
            t = V.ts(n, n, -12582912.0, None, ALU.add, w=(t,))
            for c in (6.28125, 0.0019350051879882812, 3.0199e-07):
                t = V.stt(ang, n, -c, ang, ALU.mult, ALU.add, w=(t,))
            t = V.ts(ang, ang, 3.1415925, -3.1415925, ALU.min, ALU.max, w=(t,))
            cs, sn = cos_t[:, 0:512], cos_t[:, 512:1024]
            t1 = A.act(sn, ang, ACT.Sin, w=(t,))
            t = V.stt(r, ang, -1.0, ang, ALU.mult, ALU.max, w=(t,) + tuple(s[2].free))
            t = A.act(cs, r, ACT.Sin, w=(t,), scale=-1.0, bias=hpi)
            for x in s:
                x.give(t)
            return t

        rh = [S_t[:, 512 * c:512 * c + 512] for c in range(10)]
        rl = [S_t[:, 5120 + 512 * c:5120 + 512 * c + 512] for c in range(10)]
        rhf = [ST_t[:, 512 * c:512 * c + 512] for c in range(10)]
        rlf = [ST_t[:, 5120 + 512 * c:5120 + 512 * c + 512] for c in range(10)]
        cvh = [S_t[:, 10240 + 512 * i:10752 + 512 * i] for i in range(4)]
        cvl = [S_t[:, 12288 + 512 * i:12800 + 512 * i] for i in range(4)]
        r_tok = [None] * 10
        cv_free = [()] * 4
        staged = {}

        def rnn_in(c):
            i = c % 2
            b = bank[i]
            t = linear("w_in", 24 + c, b, Hh, Hl, h1)
            t = A.copy(pad[i][:, 32:544], b.ap, w=(t,) + tuple(pad_free[i]) + (pad0[i],))
            b.give(t)
            cv = rhf[c]
            wv = [prm("conv_w", 4 * c + j) for j in range(4)]
            t = V.ts(cv, pad[i][:, 32:544], wv[3], prm("conv_b", c), ALU.mult, ALU.add, w=(t,))
            for j in (2, 1, 0):
                t = V.stt(cv, pad[i][:, 29 + j:541 + j], wv[j], cv, ALU.mult, ALU.add, w=(t,))
            pad_free[i] = (t,)
            pt = parts(cv, cvh[c % 4], cvl[c % 4], w=(t,), free=cv_free[c % 4])
            by = bank[2 + i]
            t = linear("w_in", 34 + c, by, Hh, Hl, h1)
            gt = A.act(rlf[c], by.ap, ACT.Gelu_apprx_tanh, w=(t,))
            by.give(gt)
            staged[c] = (pt, gt)

        def rnn_out(pair):
            s = {}
            for c in pair:
                pt, gt = staged[c]
                hi, lo, wt, j = w_get("w_rg", c)
                br, bx = bank[4 + 2 * (c % 2)], bank[5 + 2 * (c % 2)]
                br.held = bx.held = True
                ch, cl = cvh[c % 4], cvl[c % 4]
                tr = P.mm3(br.ap, hi[:, 0:128], lo[:, 0:128], ch, cl, True, True,
                           w=(wt, pt) + tuple(br.free), inc=True)
                tx = P.mm3(bx.ap, hi[:, 128:256], lo[:, 128:256], ch, cl, True, True,
                           w=tuple(bx.free), inc=True)
                w_done(j, tx)
                cv_free[c % 4] = (tx,)
                r, g, m = scr.take(), scr.take(), scr.take()
                t = A.act(r.ap, br.ap, ACT.Sigmoid, w=(tr,) + tuple(r.free), bias=prm("b_rg_a", c))
                br.give(t)
                t2 = A.act(g.ap, bx.ap, ACT.Sigmoid, w=(tx,) + tuple(g.free), bias=prm("b_rg_x", c))
                bx.give(t2)
                tm = A.act(m.ap, r.ap, ACT.Tanh, w=(t,) + tuple(m.free), scale=nsp[:, c:c + 1])
                gx = V.tt(g.ap, g.ap, rhf[c], ALU.mult, w=(t2, pt))
                s[c] = [r, g, m, tm, gx]
            for c in pair:
                r, g, m, tm, gx = s[c]
                ta = A.act(r.ap, r.ap, ACT.Exp, w=(tm,), scale=nsp[:, c:c + 1])
                t = A.act(rhf[c], r.ap, ACT.Square, w=(ta, gx))
                t = V.stt(m.ap, rhf[c], 1.0, m.ap, ALU.add, ALU.mult, w=(t,))
                s[c][3:] = [ta, t]
            for c in pair:
                r, g, m, ta, t = s[c]
                t = A.act(m.ap, m.ap, ACT.Sqrt, w=(t,), scale=-1.0)
                t = V.tt(g.ap, g.ap, m.ap, ALU.mult, w=(t,))
                t = V.scan(rhf[c], r.ap, g.ap, w=(t, ta))
                r.give(t)
                g.give(t)
                m.give(t)
                t = V.tt(rlf[c], rlf[c], rhf[c], ALU.mult, w=(t, staged[c][1]))
                t = A.copy(rh[c], rlf[c], w=(t,))
                s[c] = t
            for c in pair:
                r_tok[c] = V.tt(rl[c], rlf[c], f(rh[c]), ALU.subtract, w=(s[c],))

        for c in range(0, 10, 2):
            rnn_in(c)
            rnn_in(c + 1)
            if c:
                rnn_out((c - 2, c - 1))
        rnn_out((8, 9))

        m_tok = []
        for m in range(8):
            bg, bo = bank[m % 2], bank[2 + m % 2]
            t = linear("w_in", 52 + m, bg, Hh, Hl, h1)
            s = scr.take()
            tg = A.act(s.ap, bg.ap, ACT.Sigmoid, w=(t,) + tuple(s.free), bias=prm("b_gate", 8 + m))
            bg.give(tg)
            linear("w_brr", 2 * m, bo, rh[0:5], rl[0:5], r_tok[0:5], kk=5, stop=False)
            t = linear("w_brr", 2 * m + 1, bo, rh[5:10], rl[5:10], r_tok[5:10], kk=5, start=False, take=False)
            rn_last = t
            t = V.tt(X[m], bo.ap, s.ap, ALU.mult, w=(t, tg, h1[m]))
            bo.give(t)
            s.give(t)
            m_tok.append(t)

        def region(o, n):
            return S_t[:, o:o + n]

        def regionf(o, n):
            return ST_t[:, o:o + n]

        oh = [region(512 * h, 512) for h in range(8)]
        ol = [region(4096 + 512 * h, 512) for h in range(8)]
        ohf = [regionf(512 * h, 512) for h in range(8)]
        olf = [regionf(4096 + 512 * h, 512) for h in range(8)]
        qk = [[region(8192 + 2048 * i + 512 * j, 512) for j in range(4)] for i in range(2)]
        qkf = [[regionf(8192 + 2048 * i + 512 * j, 512) for j in range(4)] for i in range(2)]
        vv = [[region(12288 + 1024 * i + 512 * j, 512) for j in range(2)] for i in range(2)]
        vvf = [[regionf(12288 + 1024 * i + 512 * j, 512) for j in range(2)] for i in range(2)]
        dts = Slots([Slot([region(14336 + 1024 * i + 512 * j, 512) for j in range(2)]) for i in range(2)])
        for s in dts.slots:
            s.free = (rn_last,)
        qk_free = [(rn_last,), (rn_last,)]
        vv_free = [(rn_last,), (rn_last,)]
        pbank = Slots([bank[0], bank[1]])
        sbank = Slots([Slot([bank[2], bank[3]]), Slot([bank[4], bank[5]])])
        for s in sbank.slots:
            s.free = tuple(t for b in s.ap for t in b.free)
        tbank, obank = bank[6], bank[7]
        small = Slots([Slot(sm_t[:, 128 + 32 * i:160 + 32 * i]) for i in range(4)])
        for s in small.slots:
            s.free = (sp_tok,)

        def group_sums(sq, tok, lhs, n=T):
            b = pbank.take()
            t = P.mm(b.ap[:, 0:n], lhs, sq[:, 0:n], True, True, w=(tok,) + tuple(b.free), inc=True)
            return b, t

        def root(b, t, width, gain=1.0, bias=None, n=T):
            r = scr.take()
            t = A.act(r.ap[:, 0:n], b.ap[:, 0:n], ACT.Sqrt, w=(t,) + tuple(r.free),
                      scale=gain / width, bias=eps if bias is None else bias)
            b.give(t)
            return r, t

        def scaled(r, t, gain, xf, n=T):
            t = V.recip(r.ap[:, 0:n], r.ap[:, 0:n], w=(t,))
            t = V.stt(xf[:, 0:n], xf[:, 0:n], gain, r.ap[:, 0:n], ALU.mult, ALU.mult, w=(t,))
            r.give(t)
            return t

        def parts_in_place(hi, lo, lof, t, w=()):
            t = A.copy(hi, lof, w=(t,) + tuple(w))
            return V.tt(lo, lof, f(hi), ALU.subtract, w=(t,))

        def raw_and_squares(b, t, xf, sqf, free, n=T):
            t1 = A.copy(xf[:, 0:n], b.ap[:, 0:n], w=(t,) + tuple(free))
            t2 = A.act(sqf[:, 0:n], b.ap[:, 0:n], ACT.Square)
            b.give(t2)
            return t2

        def rows_of(xf, t, hi, lo, n=4):
            b = pbank.take()
            for k in range(n):
                tt = P.tr(b.ap[:, 128 * k:128 * k + 128], xf[:, 128 * k:128 * k + 128], ident,
                          w=(t,) + (tuple(b.free) if k == 0 else ()), inc=k == n - 1)
            t = parts(b.ap[:, 0:128 * n], hi, lo, w=(tt,))
            b.give(t)
            return t

        ready = {}
        past = {"scores": -1, "values": -1}
        o_wait = []
        o_tok = [None] * 8

        def o_norms(b_and_r):
            for h, r, t in b_and_r:
                t = scaled(r, t, prm("subln_g"), olf[h])
                o_tok[h] = parts_in_place(oh[h], ol[h], olf[h], t)

        def o_roots():
            res = []
            while o_wait:
                h, t = o_wait.pop(0)
                b, t = group_sums(ohf[h], t, ones)
                r, t = root(b, t, 128, gain=1.0 / 0.64, bias=eps2)
                res.append((h, r, t))
            return res

        def proj():
            for h in range(8):
                i = h % 2
                q_h, q_l, k_h, k_l = qk[i]
                qf, kf = (qkf[i][1], qkf[i][0]), (qkf[i][3], qkf[i][2])
                b = pbank.take()
                t = yield from linear_g("w_in", h, b, Hh, Hl, h1)
                while past["scores"] < h - 2:
                    yield
                tq = raw_and_squares(b, t, qf[0], qf[1], qk_free[i])
                yield
                b = pbank.take()
                t = yield from linear_g("w_in", 8 + h, b, Hh, Hl, h1)
                tk = raw_and_squares(b, t, kf[0], kf[1], qk_free[i])
                yield
                bv = pbank.take()
                lv = linear_g("w_in", 16 + h, bv, Hh, Hl, h1, cuts=(2, 5))
                next(lv)
                rs = []
                for x, sq in ((tq, qf[1]), (tk, kf[1])):
                    b, t = group_sums(sq, x, blk)
                    rs.append(root(b, t, 64))
                ors = o_roots()
                next(lv)
                t1 = scaled(*rs[0], prm("q_norm_g"), qf[0])
                t2 = scaled(*rs[1], prm("k_norm_g"), kf[0])
                t1 = parts_in_place(q_h, q_l, qf[0], t1)
                t2 = parts_in_place(k_h, k_l, kf[0], t2)
                ready[h] = [t1, t2, None]
                yield
                t = yield from lv
                while past["values"] < h - 2:
                    yield
                t = A.copy(vvf[i][1], bv.ap, w=(t,) + vv_free[i])
                bv.give(t)
                o_norms(ors)
                yield
                ready[h][2] = rows_of(vvf[i][1], t, vv[i][0], vv[i][1])

        class Item:
            pass

        def first_scores(it):
            h, qb = it.h, it.qb
            while h not in ready:
                next(side)
            tq, tk = ready[h][0:2]
            q_h, q_l, k_h, k_l = qk[h % 2]
            n = it.n = 128 * (qb + 1)
            sb = sbank.take()
            for c in range(2):
                b, r = sb.ap[c].ap, slice(64 * c, 64 * c + 64)
                P.mm3(b[:, 0:n], q_h[r, 128 * qb:128 * qb + 128], q_l[r, 128 * qb:128 * qb + 128],
                      k_h[r, 0:n], k_l[r, 0:n], True, False, w=(tq, tk) + tuple(sb.free))
                t = P.mm(b[:, n - 64:n], idb_t[:, :], m1b_t[:, :], False, True, w=(masks,), inc=True)
            if qb == 3:
                qk_free[h % 2] = (t,)
                past["scores"] = h
            soft(it, sb, t, n, None)

        def soft(it, sb, tok, n, sink):
            s = it.small = small.take()
            mx, nm, sm = (s.ap[:, 4 * i:4 * i + 2] for i in range(3))
            t1 = V.red(mx[:, 0:1], sb.ap[0].ap[:, 0:n], ALU.max, w=(tok,) + tuple(s.free))
            t = V.red(mx[:, 1:2], sb.ap[1].ap[:, 0:n], ALU.max)
            if sink is None:
                t = V.ts(nm, mx, -0.125, None, ALU.mult, w=(t,))
            else:
                t = V.stt(mx, mx, 0.125, sink, ALU.mult, ALU.max, w=(t,))
                t = V.ts(nm, mx, -1.0, None, ALU.mult, w=(t,))
            it.p = []
            for c in range(2):
                p = scr.take()
                te = A.act(p.ap[:, 0:n], sb.ap[c].ap[:, 0:n], ACT.Exp, w=(t,) + tuple(p.free),
                           scale=0.125, bias=nm[:, c:c + 1], acc=sm[:, c:c + 1])
                it.p.append(p)
            sb.give(te)
            if sink is not None:
                sk_ = s.ap[:, 12:14]
                t = V.tt(sk_, sink, nm, ALU.add, w=(t,))
                te = A.act(sk_, sk_, ACT.Exp, w=(t,))
            it.t = te

        def first_weigh(it):
            rc, sm = it.small.ap[:, 16:18], it.small.ap[:, 8:10]
            n = it.n
            t = V.recip(rc, sm, w=(it.t,))
            t = V.tt(rc[:, 1:2], rc[:, 1:2], neglam, ALU.mult, w=(t,))
            p0, p1 = it.p
            t = V.ts(p1.ap[:, 0:n], p1.ap[:, 0:n], rc[:, 1:2], None, ALU.mult, w=(t,))
            t = V.stt(p0.ap[:, 0:n], p0.ap[:, 0:n], rc[:, 0:1], p1.ap[:, 0:n], ALU.mult, ALU.add, w=(t,))
            p1.give(t)
            it.small.give(t)
            it.t = t

        def first_turn(it):
            n = it.qb + 1
            for k in range(n):
                ks = slice(128 * k, 128 * k + 128)
                t = P.tr(tbank.ap[:, ks], it.p[0].ap[:, ks], ident,
                         w=(it.t,) + (tuple(tbank.free) if k == 0 else ()), inc=k == n - 1)
            it.p[0].give(t)
            d = it.d = dts.take()
            it.t = parts(tbank.ap[:, 0:128 * n], d.ap[0][:, 0:128 * n], d.ap[1][:, 0:128 * n], w=(t,),
                         free=tuple(d.free))
            tbank.free = (it.t,)

        def first_values(it):
            h, qb, i = it.h, it.qb, it.h % 2
            while ready[h][2] is None:
                next(side)
            d = it.d
            for k in range(qb + 1):
                vs = slice(128 * k, 128 * k + 128)
                t = P.mm3(obank.ap[:, 128 * qb:128 * qb + 128], vv[i][0][:, vs], vv[i][1][:, vs],
                          d.ap[0][:, vs], d.ap[1][:, vs], k == 0, k == qb,
                          w=(it.t, ready[h][2]) + (tuple(obank.free) if qb == 0 and k == 0 else ()),
                          inc=k == qb)
            d.give(t)
            if qb == 3:
                vv_free[i] = (t,)
                past["values"] = h
                t1 = A.copy(olf[h], obank.ap, w=(t, rn_last))
                t1 = A.act(ohf[h], obank.ap, ACT.Square)
                obank.free = (t1,)
                o_wait.append((h, t1))

        def pipeline(items, fns, step):
            scores, weigh, turn, values = fns
            for n in range(len(items) + 2):
                if n >= 2:
                    turn(items[n - 2])
                if 1 <= n <= len(items):
                    weigh(items[n - 1])
                if n < len(items):
                    scores(items[n])
                step()
                if n >= 2:
                    values(items[n - 2])
                step()

        side = proj()
        items = []
        for h in range(8):
            for qb in range(4):
                it = Item()
                it.h, it.qb = h, qb
                items.append(it)
        pipeline(items, (first_scores, first_weigh, first_turn, first_values), lambda: next(side, None))
        for _ in side:
            pass
        o_norms(o_roots())
        for s in sbank.slots:
            for b in s.ap:
                b.free = tuple(s.free)

        mh, ml = ([region(8192 + 512 * m, 512) for m in range(8)],
                              [region(12288 + 512 * m, 512) for m in range(8)])
        g_tok = []
        for m in range(8):
            bg, bo = bank[m % 2], bank[2 + m % 2]
            t = linear("w_in", 44 + m, bg, Hh, Hl, h1)
            s = scr.take()
            tg = A.act(s.ap, bg.ap, ACT.Sigmoid, w=(t,) + tuple(s.free), bias=prm("b_gate", m))
            bg.give(tg)
            t = linear("w_bra", m, bo, oh, ol, o_tok)
            last_bra = t
            t = V.tt(s.ap, bo.ap, s.ap, ALU.mult, w=(t, tg))
            bo.give(t)
            t = V.tt(s.ap, s.ap, X[m], ALU.add, w=(t, m_tok[m]))
            t = parts(s.ap, mh[m], ml[m], w=(t,), free=tuple(vv_free[0]) + tuple(vv_free[1]) + tuple(qk_free[1]))
            s.give(t)
            g_tok.append(t)
        x_back = load_x((g_tok[7],))
        x1 = []
        for m in range(8):
            b = bank[m % 2]
            t = linear("w_out", m, b, mh, ml, g_tok)
            t2 = V.tt(X[m], X[m], b.ap, ALU.add, w=(t, x_back[m // 2]))
            b.give(t2)
            x1.append(t2)
        last_out = t

        def finish(toks):
            tt = S.dma(out.rearrange("(k p) t -> p k t", p=128),
                       X_t[:, :].rearrange("p (k t) -> p k t", k=8), x_sem[0], w=tuple(toks))
            S.wait((tt,))

        def peer():
            h2 = norm(X, x1, [prm("norm2_g", k) for k in range(8)], Hh, Hl, T)
            ST = ST_t[:, :]
            spill = []
            ub = Slots([bank[0], bank[1]])
            G1 = Slots([bank[4], bank[5]])

            def u_chunks():
                for i in range(128):
                    b = ub.take()
                    b.held = False
                    t = linear("pu", i, b, Hh, Hl, h2)
                    s = scr.take()
                    t = A.act(s.ap, b.ap, ACT.Gelu_apprx_tanh, w=(t,) + tuple(s.free))
                    b.give(t)
                    tt = S.dma(ad[i, :, :], s.ap, s.sem, w=(t,))
                    s.give(tt)
                    spill.append(tt)
                    yield

            qh, ql = [region(15360, 512), region(14336, 512)], [region(15872, 512), region(14848, 512)]
            q_free = [(last_out,), (last_out,)]
            vals = sm_t[:, 0:128].rearrange("p (c b k) -> p c b k", c=2, b=4)
            idxf = sm_t[:, 128:256].rearrange("p (c b k) -> p c b k", c=2, b=4)
            idxu = su_t[:, 0:128].rearrange("p (c b k) -> p c b k", c=2, b=4)
            posu = su_t[:, 128:192]
            pt = su_t[:, 192:256]
            I1, I2, TS = scr.take(), scr.take(), scr.take()
            V.wait(tuple(I1.free) + tuple(I2.free) + tuple(TS.free) + (last_out,))
            v4 = {id(z): z.ap.rearrange("p (b h k) -> p b h k", b=4, h=8) for z in (I1, I2, TS)}
            cand = ST[:, 0:1024].rearrange("p (b i j) -> p b i j", b=4, i=16)
            cand2 = ST[:, 1024:2048]
            eq = ST[:, 2048:3072].rearrange("p (b k a) -> p b k a", b=4, k=16)
            sc2 = ST[:, 3072:3200]
            pf = ST[:, 3200:3264].rearrange("p (b k) -> p b k", b=4)

            def topk():
                for h in range(8):
                    for c in range(2):
                        j = 2 * h + c
                        b = bank[2]
                        t = linear("w_pq", j, b, Hh, Hl, h2)
                        t = parts(b.ap, qh[c], ql[c], w=(t,), free=q_free[c])
                        b.give(t)
                        yield
                        yield
                        hi, lo, wt, jj = w_get("sk", j)
                        b = bank[3]
                        assert not b.held
                        b.held = True
                        for tb in range(4):
                            ts = slice(128 * tb, 128 * tb + 128)
                            t1 = P.mm3(b.ap[:, ts], qh[c][:, ts], ql[c][:, ts], hi, lo, True, True,
                                       w=(t, wt) + (tuple(b.free) if tb == 0 else ()), inc=tb == 3)
                        w_done(jj, t1)
                        q_free[c] = (t1,)
                        for tb in range(4):
                            sc = b.ap[:, 128 * tb:128 * tb + 128]
                            v, ix = vals[:, c, tb, :], idxu[:, c, tb, :]
                            t = V.max8(v[:, 0:8], sc, w=(t1,))
                            t = V.idx8(ix[:, 0:8], v[:, 0:8], sc, w=(t,))
                            t = V.rep8(sc2, v[:, 0:8], sc, w=(t,))
                            t = V.max8(v[:, 8:16], sc2, w=(t,))
                            t = V.idx8(ix[:, 8:16], v[:, 8:16], sc2, w=(t,))
                        b.give(t)
                        yield
                    t = V.copy(idxf, idxu, w=(t,))
                    s1 = vals[:, 0, :, :].unsqueeze(3).to_broadcast([128, 4, 16, 16])
                    s2 = vals[:, 1, :, :].unsqueeze(2).to_broadcast([128, 4, 16, 16])
                    for tb in range(4):
                        t = V.tt(cand[:, tb], s1[:, tb], s2[:, tb], ALU.add, w=(t,))
                    for tb in range(4):
                        cf = ST[:, 256 * tb:256 * tb + 256]
                        c2 = cand2[:, 256 * tb:256 * tb + 256]
                        top = v4[id(TS)][:, tb, h, :]
                        pu = posu[:, 16 * tb:16 * tb + 16]
                        t = V.max8(top[:, 0:8], cf, w=(t,))
                        t = V.idx8(pu[:, 0:8], top[:, 0:8], cf, w=(t,))
                        t = V.rep8(c2, top[:, 0:8], cf, w=(t,))
                        t = V.max8(top[:, 8:16], c2, w=(t,))
                        t = V.idx8(pu[:, 8:16], top[:, 8:16], c2, w=(t,))
                        if tb % 2:
                            yield
                    it = iota[:, 0:16].unsqueeze(1).to_broadcast([128, 64, 16])
                    eq3 = ST[:, 2048:3072].rearrange("p (q a) -> p q a", q=64)
                    pf2 = ST[:, 3200:3264]
                    for c, (op, imm, dst) in enumerate(((ALU.logical_shift_right, 4, I1),
                                                        (ALU.bitwise_and, 15, I2))):
                        t = V.ts(pt, posu, imm, None, op, w=(t,))
                        t = V.copy(pf2, pt, w=(t,))
                        t = V.tt(eq3, it, pf2.unsqueeze(2).to_broadcast([128, 64, 16]), ALU.is_equal, w=(t,))
                        for tb in range(4):
                            t = V.tt(eq[:, tb], eq[:, tb],
                                     idxf[:, c, tb, :].unsqueeze(1).to_broadcast([128, 16, 16]),
                                     ALU.mult, w=(t,))
                        t = V.red(v4[id(dst)][:, :, h, :], eq, ALU.add, w=(t,))
                        state["t"] = t
                        yield

            state = {}

            def experts():
                for _ in topk():
                    yield
                t = state["t"]
                ts3 = TS.ap.rearrange("p (g k) -> p g k", k=16)
                mxs = sm_t[:, 0:32]
                t = V.red(mxs, ts3, ALU.max, w=(t,))
                t = V.tt(ts3, ts3, mxs.unsqueeze(2).to_broadcast([128, 32, 16]), ALU.subtract, w=(t,))
                t = A.act(TS.ap, TS.ap, ACT.Exp, w=(t,))
                t = V.red(mxs, ts3, ALU.add, w=(t,))
                t = V.recip(mxs, mxs, w=(t,))
                t = V.tt(ts3, ts3, mxs.unsqueeze(2).to_broadcast([128, 32, 16]), ALU.mult, w=(t,))
                yield
                tk = []
                for z in (I1, I2, TS):
                    b = bank[6]
                    b.held = True
                    for tb in range(4):
                        p = P.tr(b.ap[:, 128 * tb:128 * tb + 128], z.ap[:, 128 * tb:128 * tb + 128], ident,
                                 w=(t,) + (tuple(b.free) if tb == 0 else ()), inc=tb == 3)
                    t4 = V.copy(z.ap, b.ap, w=(p,))
                    b.give(t4)
                    tk.append(t4)
                    yield
                TH = scr.take()
                th = oh_t[0][:, 512 * scr.slots.index(TH):512 * scr.slots.index(TH) + 512]
                t5 = V.copy(th, TS.ap, w=(tk[2],) + tuple(TH.free))
                t5 = V.tt(TS.ap, TS.ap, f(th), ALU.subtract, w=(t5,))
                o2 = [scr.take() for _ in range(2)]
                ohs = [Slot(oh_t[0][:, 512 * scr.slots.index(z):512 * scr.slots.index(z) + 384]) for z in o2]
                for z, s_ in zip(ohs, o2):
                    z.free = tuple(s_.free)
                ohs += [Slot(oh_t[1][:, 544 * i:544 * i + 384]) for i in range(2)]
                ohs += [Slot(oh_t[2][:, 512 * i:512 * i + 384]) for i in range(2)]
                ohs = Slots([ohs[i] for i in (0, 2, 4, 1, 3, 5)])
                stage = ST[:, :].rearrange("p (i t) -> p i t", i=128)
                st_free = (t,)
                gsem = [sem(), 0]
                for tb in range(4):
                    for g in range(32):
                        b = G1.take()
                        for u in range(4):
                            o = ohs.take()
                            tok = 128 * tb + 4 * g + u
                            oa, oh_, ol_ = (o.ap[:, 128 * i:128 * i + 128] for i in range(3))
                            ta = (G if u == 3 else V).ts(oa, iota, I1.ap[:, tok:tok + 1], None,
                                                         ALU.is_equal, w=(t5,) + tuple(o.free))
                            V.ts(oh_, iota, I2.ap[:, tok:tok + 1], f(th)[:, tok:tok + 1],
                                 ALU.is_equal, ALU.mult, w=(t5,) + tuple(o.free))
                            tl = V.ts(ol_, iota, I2.ap[:, tok:tok + 1], TS.ap[:, tok:tok + 1],
                                      ALU.is_equal, ALU.mult)
                            us = slice(128 * u, 128 * u + 128)
                            P.mm(b.ap[:, us], oh_, oa, True, False, w=(ta, tl) + tuple(b.free))
                            p = P.mm(b.ap[:, us], ol_, oa, False, True, inc=True)
                            o.give(p)
                        t = A.copy(stage[:, :, 4 * g:4 * g + 4].rearrange("p i u -> p u i"),
                                   b.ap.rearrange("p (u i) -> p u i", u=4), w=(p,) + tuple(st_free))
                        b.give(t)
                        st_free = ()
                        if g % 5 == 2:
                            yield
                    st_free = (S.dma(gd[:, :, 128 * tb:128 * tb + 128].rearrange("i p t -> p i t"), stage,
                                     gsem, w=(t,)),)
                    for _ in range(4 if tb < 3 else 0):
                        yield
                gdone.append(st_free[0])
                for z in (I1, I2, TS, TH, *o2):
                    z.give(t, p)

            gdone = []
            uc = u_chunks()
            ex = experts()
            n_u = 0
            while True:
                try:
                    next(ex)
                except StopIteration:
                    break
                if next(uc, 0) != 0:
                    n_u += 1
            ga = [Slot((ST_t[:, 8192 + 2048 * i:9216 + 2048 * i], ST_t[:, 9216 + 2048 * i:10240 + 2048 * i]),
                       [sem(), 0]) for i in range(4)]
            for s in ga:
                s.free = (gdone[0],)
            wac = [Slot((region(8192 * i, 4096), region(8192 * i + 4096, 4096))) for i in range(2)]
            for w_ in wac:
                w_.free = (gdone[0],)
            loads = []

            def ga_load(p):
                s = ga[p % 4]
                S.dma(s.ap[0].rearrange("p (i t) -> p i t", i=2),
                      gd[2 * p:2 * p + 2, :, :].rearrange("i p t -> p i t"), s.sem,
                      w=tuple(s.free) + (gdone[0], spill[2 * p], spill[2 * p + 1]))
                t = S.dma(s.ap[1].rearrange("p (i t) -> p i t", i=2),
                          ad[2 * p:2 * p + 2, :, :].rearrange("i p t -> p i t"), s.sem)
                loads.append((s, t))

            left = 128 - len(spill)
            for i in range(left - 2):
                next(uc)
            for p in range(4):
                ga_load(p)
            for _ in uc:
                pass
            last_u = (P.sem, P.n)
            for i in range(4):
                ga[i] = Slot((GA_t[:, 2048 * i:2048 * i + 1024], GA_t[:, 2048 * i + 1024:2048 * i + 2048]),
                             [sem(), 0])
                ga[i].free = (last_u,)

            x_last = list(h2)
            toks = {}

            def weigh(g):
                w_ = wac[g % 2]
                res = []
                for p in range(4):
                    s, t = loads.pop(0)
                    t = V.tt(s.ap[1], s.ap[0], s.ap[1], ALU.mult, w=(t,))
                    t = parts(s.ap[1], w_.ap[0][:, 1024 * p:1024 * p + 1024],
                              w_.ap[1][:, 1024 * p:1024 * p + 1024], w=(t,), free=tuple(w_.free))
                    s.free = (t,)
                    if 4 * g + p + 4 < 64:
                        ga_load(4 * g + p + 4)
                    res.append(t)
                    yield
                toks[g] = res

            for _ in weigh(0):
                pass
            wac[1].free = (toks[0][3],)
            for g in range(16):
                nxt = weigh(g + 1) if g < 15 else iter(())
                w_ = wac[g % 2]
                for half in range(2):
                    bs = [bank[4 * half + d] for d in range(4)]
                    for b in bs:
                        assert not b.held
                        b.held = True
                    for p in range(4):
                        hi, lo, t, j = w_get("pv", (g * 2 + half) * 4 + p)
                        for i in range(2):
                            for d in range(4):
                                ws = slice(512 * i + 128 * d, 512 * i + 128 * d + 128)
                                rs = slice(1024 * p + 512 * i, 1024 * p + 512 * i + 512)
                                last = P.mm3(bs[d].ap, hi[:, ws], lo[:, ws], w_.ap[0][:, rs], w_.ap[1][:, rs],
                                             p == 0 and i == 0, p == 3 and i == 1,
                                             w=(t, toks[g][p]) + (tuple(bs[d].free) if p == 0 and i == 0 else ()),
                                             inc=p == 3 or (i == 1 and d == 3))
                                if p == 3 and i == 1:
                                    bs[d].give(last)
                        w_done(j, last)
                        next(nxt, None)
                    for d in range(4):
                        k = 4 * half + d
                        x_last[k] = V.tt(X[k], X[k], bs[d].ap, ALU.add, w=tuple(bs[d].free) + (x_last[k],))
                        bs[d].free = (x_last[k],)
                w_.free = (last,)
                for _ in nxt:
                    pass
            return x_last

        def u_last(q):
            return (q.sem, q.n)

        oa_t, ob_t = pad_t, cos_t

        def ffn(tag, gname, xt):
            s_free0 = u_last(P)
            hx = norm(X, xt, [prm(gname, k) for k in range(8)], Hh, Hl, T, free=(s_free0,))
            sl = Slots([Slot((region(1024 * i, 512), region(1024 * i + 512, 512))) for i in range(16)])
            for s in sl.slots:
                s.free = (s_free0,)
            held = {}
            gi_b, up_b = Slots([bank[0], bank[1]]), Slots([bank[2], bank[3]])

            def hidden(i):
                b = gi_b.take()
                b.held = False
                t = linear("wg" + tag, i, b, Hh, Hl, hx)
                s = scr.take()
                ts_ = A.act(s.ap, b.ap, ACT.Silu, w=(t,) + tuple(s.free))
                b.give(ts_)
                b = up_b.take()
                b.held = False
                t = linear("wu" + tag, i, b, Hh, Hl, hx)
                t = V.tt(s.ap, s.ap, b.ap, ALU.mult, w=(t, ts_))
                b.give(t)
                z = sl.take()
                t = parts(s.ap, z.ap[0], z.ap[1], w=(t,), free=tuple(z.free))
                s.give(t)
                held[i] = (z, t)

            xl = list(xt)
            down_b = Slots([bank[4], bank[5], bank[6]])
            for gi in range(4):
                if gi < 3:
                    for i in range(FG[gi][0], sum(FG[gi])):
                        hidden(i)
                if gi > 0:
                    first, n = FG[gi - 1]
                    zs = [held.pop(first + i) for i in range(n)]
                    for m in range(8):
                        b = down_b.take()
                        b.held = False
                        t = linear("wd" + tag, (gi - 1) * 8 + m, b, [z[0].ap[0] for z in zs],
                                   [z[0].ap[1] for z in zs], [z[1] for z in zs], kk=n)
                        t2 = V.stt(X[m], b.ap, 0.5, X[m], ALU.mult, ALU.add, w=(t, xl[m], hx[7]))
                        b.give(t2)
                        xl[m] = t2
                    for z in zs:
                        z[0].give(t)
            return xl

        def mixer(xt):
            p0 = u_last(P)
            rope_tok = rope_tables()
            for i in range(2):
                pad_free[i] = (V.fill(pad[i][:, 0:32], 0.0),)
            ms = [scr.take() for _ in range(4)]
            mt = [S.dma(ms[i].ap.rearrange("p (k t) -> p k t", k=2), a["mem"][:, 2 * i:2 * i + 2, :], ms[i].sem,
                        w=tuple(ms[i].free)) for i in range(4)]
            hx = norm(X, xt, [prm("g_mix_2", k) for k in range(8)], Hh, Hl, T, free=(p0,))
            yh = [region(512 * c, 512) for c in range(8)]
            yl = [region(4096 + 512 * c, 512) for c in range(8)]
            yhf = [regionf(512 * c, 512) for c in range(8)]
            ylf = [regionf(4096 + 512 * c, 512) for c in range(8)]
            kh, kl, vh, vl = (region(8192 + 512 * i, 512) for i in range(4))
            khf, klf, vhf, vlf = (regionf(8192 + 512 * i, 512) for i in range(4))
            qs = Slots([Slot([z(10240 + 1024 * i + 512 * j, 512) for z in (region, regionf) for j in range(2)])
                        for i in range(2)])
            mkh, mkl, mvh, mvl = ([region(12288 + 512 * j + 256 * c, 256) for c in range(2)] for j in range(4))
            mkhf, mklf, mvhf, mvlf = ([regionf(12288 + 512 * j + 256 * c, 256) for c in range(2)] for j in range(4))
            for s in dts.slots + qs.slots:
                s.free = (p0,)
            y_tok = [None] * 8

            b = pbank.take()
            t = yield_all(linear_g("w_in2", 4, b, Hh, Hl, hx))
            tk0 = raw_and_squares(b, t, klf, khf, (p0,))
            b = pbank.take()
            t = yield_all(linear_g("w_in2", 5, b, Hh, Hl, hx))
            tv0 = A.copy(vlf, b.ap, w=(t, p0))
            b.give(tv0)
            kb, kt = group_sums(khf, tk0, blk)
            kr = root(kb, kt, 64)

            def turned_by_position(tok, xf, n7):
                t3 = P.mm(n7.ap, perm, xf, True, True, w=(tok,) + tuple(n7.free), inc=True)
                s = scr.take()
                t4 = V.tt(s.ap, n7.ap, cos_t[:, 512:1024], ALU.mult, w=(t3, rope_tok) + tuple(s.free))
                n7.give(t4)
                t2 = V.tt(xf, xf, cos_t[:, 0:512], ALU.mult, w=(t3,))
                t2 = V.tt(xf, xf, s.ap, ALU.add, w=(t2, t4))
                s.give(t2)
                return t2

            cy = []
            for c in range(2):
                b = pbank.take()
                t = yield_all(linear_g("w_in2", 6 + c, b, Hh, Hl, hx))
                b2 = pbank.take()
                if c == 0:
                    kt = scaled(*kr, prm("g_k_2"), klf)
                t2 = yield_all(linear_g("w_in2", 8 + c, b2, Hh, Hl, hx))
                s = scr.take()
                ts_ = A.act(s.ap, b2.ap, ACT.Sigmoid, w=(t2,) + tuple(s.free))
                b2.give(ts_)
                tp = V.tt(pad[c][:, 32:544], s.ap, b.ap, ALU.mult, w=(t, ts_) + tuple(pad_free[c]))
                b.give(tp)
                s.give(tp)
                cy.append(tp)
                if c == 0:
                    kt = turned_by_position(kt, klf, pbank.take())
                    k_tok = parts_in_place(kh, kl, klf, kt)
                    v_tok = rows_of(vlf, tv0, vh, vl)

            chunks = [ms[k // 2].ap[:, 256 * (k % 2):256 * (k % 2) + 256] for k in range(8)]
            nh = [region(256 * k, 256) for k in range(8)]
            nl = [region(2048 + 256 * k, 256) for k in range(8)]

            def q_proj(i):
                b = pbank.take()
                t = yield from linear_g("w_in2", (0, 1, 2, 3, 10, 11)[i], b, Hh, Hl, hx, cuts=(3, 6))
                qd = qs.take()
                q_h, q_l, qhf, qlf = qd.ap
                t = raw_and_squares(b, t, qlf, qhf, qd.free)
                yield
                b, t = group_sums(qhf, t, blk)
                r, t = root(b, t, 64)
                yield
                t = scaled(r, t, prm("g_q_2") if i < 4 else prm("g_mq_2"), qlf)
                yield
                if i < 4:
                    t = turned_by_position(t, qlf, pbank.take())
                    yield
                queries[i] = (qd, parts_in_place(q_h, q_l, qlf, t))
                yield

            queries = {}
            yield_all(q_proj(0))
            hm = norm(chunks, [mt[k // 2] for k in range(8)], [prm("g_mem_2", k) for k in range(8)], nh, nl, 256,
                      free=(p0,))
            for s in ms:
                s.give(hm[7])
            tmk = []
            for c in range(4):
                b = pbank.take()
                t = yield_all(linear_g("w_mkv", c, b, nh, nl, hm, n=256))
                if c < 2:
                    tmk.append(raw_and_squares(b, t, mklf[c], mkhf[c], (p0,), n=256))
                else:
                    t = A.copy(mvlf[c - 2], b.ap[:, 0:256], w=(t, p0))
                    b.give(t)
                    tmk.append(t)
            mem_done = (P.sem, P.n)
            mk_tok, mv_tok = [None] * 2, [None] * 2

            def mem_keys():
                for c in range(2):
                    b, t = group_sums(mkhf[c], tmk[c], blk, n=256)
                    r, t = root(b, t, 64, n=256)
                    yield
                    t = scaled(r, t, prm("g_mk_2"), mklf[c], n=256)
                    mk_tok[c] = parts_in_place(mkh[c], mkl[c], mklf[c], t)
                    mv_tok[c] = rows_of(mvlf[c], tmk[2 + c], mvh[c], mvl[c], n=2)
                    yield

            def conv():
                toks = []
                for c in range(2):
                    y, t = ylf[4 + c], cy[c]
                    wd = [prm("w_dw_2", 31 * c + j) for j in range(31)]
                    t = V.ts(y, pad[c][:, 32:544], wd[30], prm("b_dw_2", c), ALU.mult, ALU.add,
                             w=(t, mem_done))
                    for j in range(30):
                        t = V.stt(y, pad[c][:, 2 + j:514 + j], wd[j], y, ALU.mult, ALU.add, w=(t,))
                        if j % 2:
                            yield
                    toks.append(t)
                b = pbank.take()
                for c in range(2):
                    p = P.mm(b.ap, ones, ylf[4 + c], c == 0, c == 1, w=(toks[c],) + tuple(b.free), inc=True)
                yield
                for c in range(2):
                    y = ylf[4 + c]
                    t = V.stt(y, b.ap, -1.0 / 256, y, ALU.mult, ALU.add, w=(p,))
                    toks[c] = A.act(yhf[4 + c], y, ACT.Square, w=(t, mem_done))
                b.give(t)
                yield
                b = pbank.take()
                for c in range(2):
                    p = P.mm(b.ap, ones, yhf[4 + c], c == 0, c == 1, w=(toks[c],) + tuple(b.free), inc=True)
                r, t = root(b, p, 256)
                yield
                rt = V.recip(r.ap, r.ap, w=(t,))
                for c in range(2):
                    y = ylf[4 + c]
                    t = V.stt(y, y, prm("g_conv_ln_2", c), r.ap, ALU.mult, ALU.mult, w=(rt,))
                    t1 = A.act(y, y, ACT.Silu, w=(t,), bias=prm("b_conv_ln_2", c))
                    y_tok[4 + c] = parts_in_place(yh[4 + c], yl[4 + c], y, t1)
                r.give(t)

            vt = ([vh[:, 128 * k:128 * k + 128] for k in range(4)], [vl[:, 128 * k:128 * k + 128] for k in range(4)])

            def chain(*gens):
                for g in gens:
                    yield from g

            side2 = chain(mem_keys(), *(q_proj(i) for i in range(1, 6)))
            cv = conv()
            for s in sbank.slots:
                s.free = tuple(t for b in s.ap for t in b.free)

            def second_scores(it):
                i, qb = it.i, it.qb
                while i not in queries:
                    next(side2)
                qd, q_tok = queries[i]
                it.local = i < 4
                it.lo_k = 0 if not it.local or qb == 0 else 128 * (qb - 1)
                n = it.n = 256 if not it.local or qb else 128
                if it.local:
                    k2, kt2 = (kh, kl), k_tok
                else:
                    while mk_tok[i - 4] is None:
                        next(side2)
                    k2, kt2 = (mkh[i - 4], mkl[i - 4]), mk_tok[i - 4]
                sb = sbank.take()
                qs_ = slice(128 * qb, 128 * qb + 128)
                ks = slice(it.lo_k, it.lo_k + n)
                for e in range(2):
                    r = slice(64 * e, 64 * e + 64)
                    b = sb.ap[e].ap
                    t = P.mm3(b[:, 0:n], qd.ap[0][r, qs_], qd.ap[1][r, qs_], k2[0][r, ks], k2[1][r, ks],
                              True, not it.local, w=(q_tok, kt2) + tuple(sb.free), inc=not it.local)
                    if it.local:
                        t = P.mm(b[:, 0:n], idb_t[:, :], m2b_t[:, 256 - n:256], False, True,
                                 w=(masks,), inc=True)
                if qb == 3:
                    qd.give(t)
                soft(it, sb, t, n, prm("sinks_2", 2 * i, 2) if it.local else None)

            def second_weigh(it):
                rc, sm, sk_ = it.small.ap[:, 16:18], it.small.ap[:, 8:10], it.small.ap[:, 12:14]
                n, t = it.n, it.t
                if it.local:
                    t = V.tt(sm, sm, sk_, ALU.add, w=(t,))
                t = V.recip(rc, sm, w=(t,))
                for e in range(2):
                    p = it.p[e].ap[:, 0:n]
                    t1 = V.ts(p, p, rc[:, e:e + 1], None, ALU.mult, w=(t,))
                it.small.give(t1)
                it.t = t1

            def second_turn(it):
                nb = it.n // 128
                for e in range(2):
                    for k in range(nb):
                        col = 256 * e + 128 * k
                        t = P.tr(tbank.ap[:, col:col + 128], it.p[e].ap[:, 128 * k:128 * k + 128], ident,
                                 w=(it.t,) + (tuple(tbank.free) if e == 0 and k == 0 else ()), inc=True)
                    it.p[e].give(t)
                d = it.d = dts.take()

                def v2(z):
                    return z.rearrange("p (e k) -> p e k", e=2)[:, :, 0:it.n]
                it.t = parts(v2(tbank.ap), v2(d.ap[0]), v2(d.ap[1]), w=(t,), free=tuple(d.free))
                tbank.free = (it.t,)

            o_free = [tuple(obank.free)] * 2

            def second_values(it):
                i, qb, d = it.i, it.qb, it.d
                if it.local:
                    vals_, vtk = vt, v_tok
                else:
                    c = i - 4
                    vals_ = tuple([z[c][:, 128 * k:128 * k + 128] for k in range(2)] for z in (mvh, mvl))
                    vtk = mv_tok[c]
                nb = it.n // 128
                half = qb % 2
                for e in range(2):
                    ocol = 256 * half + 128 * e
                    for k in range(nb):
                        vi = it.lo_k // 128 + k
                        cs = slice(256 * e + 128 * k, 256 * e + 128 * k + 128)
                        t = P.mm3(obank.ap[:, ocol:ocol + 128], vals_[0][vi], vals_[1][vi],
                                  d.ap[0][:, cs], d.ap[1][:, cs], k == 0, k == nb - 1,
                                  w=(it.t, vtk) + o_free[half], inc=k == nb - 1)
                d.give(t)
                row = it.row
                qs_ = slice(128 * qb, 128 * qb + 128)
                A.copy(ylf[row][0:64, qs_], obank.ap[0:64, 256 * half:256 * half + 128], w=(t, mem_done))
                t = A.copy(ylf[row][64:128, qs_], obank.ap[64:128, 256 * half + 128:256 * half + 256])
                o_free[half] = (t,)
                if qb == 3:
                    y_tok[row] = parts_in_place(yh[row], yl[row], ylf[row], t, w=(mem_done,))

            items = []
            for i in range(6):
                for qb in range(4):
                    it = Item()
                    it.i, it.qb, it.row = i, qb, i if i < 4 else i + 2
                    items.append(it)

            def step2():
                next(side2, None)
                next(cv, None)

            pipeline(items, (second_scores, second_weigh, second_turn, second_values), step2)
            for _ in side2:
                pass
            for _ in cv:
                pass
            obank.free = o_free[0] + o_free[1]
            for s in sbank.slots:
                for b in s.ap:
                    b.free = tuple(s.free)
            xl = []
            for m in range(8):
                b = bank[m % 2]
                t = linear("w_out2", m, b, yh, yl, y_tok)
                t2 = V.tt(X[m], X[m], b.ap, ALU.add, w=(t, hx[7]))
                b.give(t2)
                xl.append(t2)
            return xl

        def tail():
            if stop_after == "first":
                return x1
            x2 = peer()
            if stop_after == "peer":
                return x2
            x3 = ffn("1", "g_ffn1_2", x2)
            if stop_after == "ffn1":
                return x3
            x4 = mixer(x3)
            if stop_after == "mix":
                return x4
            return ffn("2", "g_ffn2_2", x4)

        finish(tail())

        block = ctx.enter_context(nc.Block())

        @block.sync
        def _(eng):
            S.emit(eng)

        @block.scalar
        def _(eng):
            A.emit(eng)

        @block.vector
        def _(eng):
            V.emit(eng)

        @block.gpsimd
        def _(eng):
            G.emit(eng)

        @block.tensor
        def _(eng):
            P.emit(eng)


def _layout(inputs):
    import numpy as np
    z = {k: np.asarray(v) for k, v in inputs.items()}
    f32 = np.float32

    def tiles(w):
        k, n = w.shape
        return np.ascontiguousarray(
            w.reshape(k // 128, 128, n // 128, 128).transpose(2, 1, 0, 3).reshape(n // 128, 128, k))

    def cols(v):
        v = v.reshape(-1)
        if v.size < 128:
            v = np.tile(v, 128 // v.size)
        return v.reshape(-1, 128).T

    d = {}
    d["x"] = np.ascontiguousarray(z["x"][0].T.reshape(8, 128, T).transpose(1, 0, 2))
    d["mem"] = np.ascontiguousarray(z["mem_2"][0].T.reshape(8, 128, 256).transpose(1, 0, 2))
    d["pos"] = np.ascontiguousarray(np.broadcast_to(z["positions_2"][0], (128, T)))
    d["lambdas"] = np.ascontiguousarray(np.broadcast_to(np.concatenate(
        [z[n][0] for n in ("lambda_q1", "lambda_k1", "lambda_q2", "lambda_k2")]), (128, 256)))
    d["w_in"] = tiles(z["w_in"][0])
    wa, wx = z["w_rg_a"][0], z["w_rg_x"][0]
    rg = np.zeros((10, 128, 256), f32)
    for c in range(10):
        for j, w in enumerate((wa, wx)):
            rg[c, 0:64, 128 * j:128 * j + 64] = w[2 * c]
            rg[c, 64:128, 128 * j + 64:128 * j + 128] = w[2 * c + 1]
    d["w_rg"] = rg
    d["w_brr"] = np.ascontiguousarray(
        tiles(z["w_br_rnn"][0]).reshape(8, 128, 2, 640).transpose(0, 2, 1, 3).reshape(16, 128, 640))
    d["w_bra"] = tiles(z["w_br_attn"][0])
    d["w_out"] = tiles(z["w_out"][0])
    d["w_pq"] = tiles(z["w_peer_q"][0])
    d["sk"] = np.ascontiguousarray(z["peer_sub_keys"][0].reshape(16, 128, 128).transpose(0, 2, 1))
    d["pu"] = np.ascontiguousarray(
        z["peer_u"][0].reshape(128, 128, 8, 128).transpose(0, 3, 2, 1).reshape(128, 128, 1024))
    d["pv"] = np.ascontiguousarray(
        z["peer_v"][0].reshape(16, 4, 2, 128, 2, 512).transpose(0, 4, 1, 3, 2, 5).reshape(128, 128, 1024))
    for fo, nm in (("1", "ffn1"), ("2", "ffn2")):
        d["wg" + fo] = tiles(z[f"w_{nm}_gate_2"][0])
        d["wu" + fo] = tiles(z[f"w_{nm}_up_2"][0])
        wd = tiles(z[f"w_{nm}_down_2"][0])
        full = np.zeros((24, 128, 1024), f32)
        for gi, (first, n) in enumerate(FG):
            full[8 * gi:8 * gi + 8, :, 0:128 * n] = wd[:, :, 128 * first:128 * (first + n)]
        d["wd" + fo] = full
    w2 = z["w_in_2"][0]
    order = [h for c in range(4) for h in (c, c + 4)]
    q2 = w2[:, 0:512].reshape(D, 8, 64)[:, order].reshape(D, 512)
    d["w_in2"] = tiles(np.concatenate([q2, w2[:, 512:]], axis=1))
    wo = z["w_out_2"][0]
    d["w_out2"] = tiles(np.concatenate([wo[0:512].reshape(8, 64, D)[order].reshape(512, D), wo[512:]], axis=0))
    d["w_mkv"] = tiles(z["w_mem_kv_2"][0])
    p = np.zeros((128, NP), f32)

    def setc(name, v):
        p[:, PCOLS[name]:PCOLS[name] + v.shape[1]] = v

    for n in ("norm1_g", "b_gate", "q_norm_g", "k_norm_g", "subln_g", "conv_b", "b_rg_a", "b_rg_x", "rg_lambda",
              "norm2_g", "g_ffn1_2", "g_mix_2", "g_q_2", "g_k_2", "b_dw_2", "g_conv_ln_2", "b_conv_ln_2",
              "g_mem_2", "g_mq_2", "g_mk_2", "g_ffn2_2"):
        setc(n, cols(z[n][0]))
    setc("conv_w", z["conv_w"][0].T.reshape(10, 128, 4).transpose(1, 0, 2).reshape(128, 40))
    setc("w_dw_2", z["w_dw_2"][0].T.reshape(2, 128, 31).transpose(1, 0, 2).reshape(128, 62))
    setc("sinks_2", np.broadcast_to(z["sinks_2"][0][order], (128, 8)))
    d["prm"] = p
    c = np.zeros((128, NC_), f32)
    i = np.arange(128)
    c[:, C_ID:C_ID + 128] = np.eye(128)
    c[:, C_ONE:C_ONE + 128] = 1
    c[:, C_BLK:C_BLK + 128] = (i[:, None] // 64) == (i[None, :] // 64)
    c[:, C_IOTA:C_IOTA + 128] = i[None, :]
    for b in (0, 64):
        for j in range(8):
            c[b + j + 8, C_PERM + b + j] = -1
            c[b + j, C_PERM + b + j + 8] = 1
            c[b + j, C_INVF] = c[b + j + 8, C_INVF] = INV_FREQ[j]
    c[:, C_MASK2:C_MASK2 + 128] = np.where(i[None, :] > i[:, None], 0, -1e30)
    c[:, C_MASK2 + 128:C_MASK2 + 256] = np.where(i[None, :] <= i[:, None], 0, -1e30)
    c[0:64, C_MASK1:C_MASK1 + 64] = -1e30
    c[:, C_EPS] = EPS
    c[:, C_EPS2] = EPS / 0.64
    c[:, C_HPI] = np.pi / 2
    d["cst"] = c
    return d


def kernel(**inputs):
    import numpy as _np
    import concourse.bacc as _bacc
    from concourse import mybir as _mybir
    from concourse.bass_utils import run_bass_kernel_spmd as _run

    nc = _bacc.Bacc("TRN2", target_bir_lowering=False, num_devices=1)
    arrays, args = {}, {}
    for name, v in _layout(inputs).items():
        v = _np.ascontiguousarray(v)
        arrays[f"in_{name}"] = v
        args[name] = nc.dram_tensor(f"in_{name}", v.shape, _mybir.dt.from_np(v.dtype), kind="ExternalInput").ap()
    out = nc.dram_tensor("out_x", (D, T), F32, kind="ExternalOutput").ap()
    build(nc, args, out)
    r = _run(nc, [arrays], core_ids=[0])
    return _np.ascontiguousarray(r.results[0]["out_x"].T).reshape(1, T, D)
```
